# Optimizing a Trainium2 kernel written in Bass

```python
import math
import jax, jax.numpy as jnp
from jax import lax
import numpy as np

D_MODEL = 1024
BATCH = 1
SEQ = 512
DEPTH = 2

N_MIXERS = 2
HEAD_DIM = 128
N_MAIN_HEADS = 12
N_MEM_HEADS = 4
N_MEM = 256
INNER = (N_MAIN_HEADS + N_MEM_HEADS) * HEAD_DIM
MAIN_W = N_MAIN_HEADS * HEAD_DIM
MEM_W = N_MEM_HEADS * HEAD_DIM
RET_KEY_DIM = HEAD_DIM // 2
BLOCK_Q = 128
RET_CHUNK = 128
ROPE_BASE = 10000.0
EPS = 1e-6
NEG = -1e30
FOX_IN = 3 * MAIN_W + N_MAIN_HEADS + MEM_W + INNER
RET_IN = 2 * N_MAIN_HEADS * RET_KEY_DIM + MAIN_W + MEM_W + INNER
N_FOX = len(range(0, DEPTH, N_MIXERS))
N_RET = len(range(1, DEPTH, N_MIXERS))


def rmsnorm(x, g):
    xf = x.astype(jnp.float32)
    y = xf * lax.rsqrt(jnp.mean(xf * xf, axis=-1, keepdims=True) + EPS)
    return (y * g.astype(jnp.float32)).astype(x.dtype)

def split_cols(t, sizes):
    idx = list(np.cumsum(sizes)[:-1])
    return jnp.split(t, idx, axis=-1)

def rotary(t, pos):
    half = t.shape[-1] // 2
    inv = 1.0 / (ROPE_BASE ** (jnp.arange(half, dtype=jnp.float32) / half))
    ang = pos[:, None] * inv[None, :]
    cos = jnp.cos(ang)[None, :, None, :].astype(t.dtype)
    sin = jnp.sin(ang)[None, :, None, :].astype(t.dtype)
    t1, t2 = t[..., :half], t[..., half:]
    return jnp.concatenate([t1 * cos - t2 * sin, t1 * sin + t2 * cos], axis=-1)

def fox_attention(q, k, v, f_logit, b_f):
    B, S, _ = q.shape
    H, d = N_MAIN_HEADS, HEAD_DIM
    q = q.reshape(B, S, H, d).transpose(0, 2, 1, 3)
    k = k.reshape(B, S, H, d).transpose(0, 2, 1, 3)
    v = v.reshape(B, S, H, d).transpose(0, 2, 1, 3)
    log_f = jax.nn.log_sigmoid(f_logit.astype(jnp.float32) + b_f.astype(jnp.float32))
    c = jnp.cumsum(log_f, axis=1).transpose(0, 2, 1)
    nb = S // BLOCK_Q
    qb = q.reshape(B, H, nb, BLOCK_Q, d).transpose(2, 0, 1, 3, 4)
    cb = c.reshape(B, H, nb, BLOCK_Q).transpose(2, 0, 1, 3)
    starts = jnp.arange(nb, dtype=jnp.int32) * BLOCK_Q
    key_pos = jnp.arange(S, dtype=jnp.int32)
    scale = 1.0 / math.sqrt(d)

    def block(args):
        qi, ci, st = args
        qpos = st + jnp.arange(BLOCK_Q, dtype=jnp.int32)
        s = jnp.einsum('bhqd,bhkd->bhqk', qi, k).astype(jnp.float32) * scale
        s = s + ci[..., None] - c[:, :, None, :]
        mask = key_pos[None, :] <= qpos[:, None]
        s = jnp.where(mask[None, None], s, NEG)
        p = jax.nn.softmax(s, axis=-1).astype(v.dtype)
        return jnp.einsum('bhqk,bhkd->bhqd', p, v)

    out = lax.map(block, (qb, cb, starts))
    return out.transpose(1, 0, 3, 2, 4).reshape(B, S, H * d)

def retention(q, k, v):
    B, S, _ = q.shape
    H, dk, dv, C = N_MAIN_HEADS, RET_KEY_DIM, HEAD_DIM, RET_CHUNK
    pos = jnp.arange(S, dtype=jnp.float32)
    qf = rotary(q.reshape(B, S, H, dk).astype(jnp.float32), pos)
    kf = rotary(k.reshape(B, S, H, dk).astype(jnp.float32), pos) * (dk ** -0.5)
    vf = v.reshape(B, S, H, dv).astype(jnp.float32)
    lg = jnp.log1p(-jnp.exp2(-5.0 - jnp.arange(H, dtype=jnp.float32)))
    n = jnp.arange(C, dtype=jnp.float32)
    diff = n[:, None] - n[None, :]
    d_inner = jnp.where(diff[None] >= 0, jnp.exp(lg[:, None, None] * jnp.maximum(diff, 0.0)[None]), 0.0)
    xi = jnp.exp(lg[:, None] * (n[None, :] + 1.0))
    zeta = jnp.exp(lg[:, None] * (C - 1.0 - n[None, :]))
    g_chunk = jnp.exp(lg * C)
    nc = S // C

    def to_chunks(t):
        return t.reshape(B, nc, C, H, t.shape[-1]).transpose(1, 0, 3, 2, 4)

    def step(R, xs):
        qc, kc, vc = xs
        inner = jnp.einsum('bhnd,bhmd->bhnm', qc, kc) * d_inner[None]
        o = jnp.einsum('bhnm,bhme->bhne', inner, vc)
        o = o + jnp.einsum('bhnd,bhde->bhne', qc, R) * xi[None, :, :, None]
        R = g_chunk[None, :, None, None] * R + jnp.einsum('bhmd,bhme->bhde', kc * zeta[None, :, :, None], vc)
        return R, o

    R0 = jnp.zeros((B, H, dk, dv), jnp.float32)
    _, out = lax.scan(step, R0, (to_chunks(qf), to_chunks(kf), to_chunks(vf)))
    out = out.transpose(1, 0, 3, 2, 4).reshape(B, S, H, dv)
    out = out * lax.rsqrt(jnp.mean(out * out, axis=-1, keepdims=True) + EPS)
    return out.reshape(B, S, H * dv).astype(q.dtype)

def mem_cross_attention(q_mem, mem_n, w_kv):
    B, S, _ = q_mem.shape
    kv = mem_n @ w_kv
    km, vm = split_cols(kv, [MEM_W, MEM_W])
    q = q_mem.reshape(B, S, N_MEM_HEADS, HEAD_DIM)
    km = km.reshape(B, -1, N_MEM_HEADS, HEAD_DIM)
    vm = vm.reshape(B, -1, N_MEM_HEADS, HEAD_DIM)
    s = jnp.einsum('bshd,bmhd->bhsm', q, km).astype(jnp.float32) / math.sqrt(HEAD_DIM)
    p = jax.nn.softmax(s, axis=-1).astype(vm.dtype)
    return jnp.einsum('bhsm,bmhd->bshd', p, vm).reshape(B, S, MEM_W)

def first_inputs(seed: int = 0) -> dict:
    key = jax.random.key(seed)
    ks = jax.random.split(key, 10)
    f32 = jnp.float32
    x = jax.random.normal(ks[0], (BATCH, SEQ, D_MODEL), f32)
    mem = jax.random.normal(ks[1], (BATCH, N_MEM, D_MODEL), f32)
    norm_g = 1.0 + 0.02 * jax.random.normal(ks[2], (DEPTH, D_MODEL), f32)
    fox_w_in = jax.random.normal(ks[3], (N_FOX, D_MODEL, FOX_IN), f32) * D_MODEL ** -0.5
    fox_b_f = 3.0 + 0.5 * jax.random.normal(ks[4], (N_FOX, N_MAIN_HEADS), f32)
    ret_w_in = jax.random.normal(ks[5], (N_RET, D_MODEL, RET_IN), f32) * D_MODEL ** -0.5
    mem_norm_g = 1.0 + 0.02 * jax.random.normal(ks[6], (D_MODEL,), f32)
    w_mem_kv = jax.random.normal(ks[7], (DEPTH, D_MODEL, 2 * MEM_W), f32) * D_MODEL ** -0.5
    w_out = jax.random.normal(ks[8], (DEPTH, INNER, D_MODEL), f32) * INNER ** -0.5
    final_norm_g = 1.0 + 0.02 * jax.random.normal(ks[9], (D_MODEL,), f32)
    return {"x": x, "mem": mem, "norm_g": norm_g, "fox_w_in": fox_w_in, "fox_b_f": fox_b_f,
            "ret_w_in": ret_w_in, "mem_norm_g": mem_norm_g, "w_mem_kv": w_mem_kv,
            "w_out": w_out, "final_norm_g": final_norm_g}

def first_block(x, mem, norm_g, fox_w_in, fox_b_f, ret_w_in, mem_norm_g, w_mem_kv, w_out, final_norm_g):
    mem_n = rmsnorm(mem, mem_norm_g)
    for i in range(DEPTH):
        h = rmsnorm(x, norm_g[i])
        j = i // N_MIXERS
        if i % N_MIXERS == 0:
            proj = h @ fox_w_in[j]
            q, k, v, f_logit, q_mem, z = split_cols(
                proj, [MAIN_W, MAIN_W, MAIN_W, N_MAIN_HEADS, MEM_W, INNER])
            main = fox_attention(q, k, v, f_logit, fox_b_f[j])
        else:
            proj = h @ ret_w_in[j]
            qk_w = N_MAIN_HEADS * RET_KEY_DIM
            q, k, v, q_mem, z = split_cols(proj, [qk_w, qk_w, MAIN_W, MEM_W, INNER])
            main = retention(q, k, v)
        memo = mem_cross_attention(q_mem, mem_n, w_mem_kv[i])
        o = jnp.concatenate([main, memo], axis=-1) * jax.nn.silu(z)
        x = x + o @ w_out[i]
    return rmsnorm(x, final_norm_g)


DEPTH_2 = 1

CHUNK = 64
CONV_A_GROUPS = 8
CONV_A_GROUP_DIM = D_MODEL // 16
CONV_A_DIM = CONV_A_GROUPS * CONV_A_GROUP_DIM
CONV_A_WIDTH = 3
DN_HEADS = 4
DN_HEAD_DIM = D_MODEL // 8
DN_DIM = DN_HEADS * DN_HEAD_DIM
DN_CONV_WIDTH = 4
MIX_DIM = CONV_A_DIM + DN_DIM
IN_PROJ_DIM = 3 * CONV_A_DIM + 4 * DN_DIM + 2 * DN_HEADS
N_GROUPS = 4
EXPERTS_PER_GROUP = 8
N_EXPERTS = N_GROUPS * EXPERTS_PER_GROUP
TOP_K = 2
EXPERT_FF = D_MODEL // 2
MOE_BLOCK = 128


def rms_norm(x, g):
    xf = x.astype(jnp.float32)
    y = xf * lax.rsqrt(jnp.mean(xf * xf, axis=-1, keepdims=True) + EPS)
    return (y * g.astype(jnp.float32)).astype(x.dtype)

def causal_dwconv(x, w):
    K = w.shape[0]
    S = x.shape[1]
    xp = jnp.pad(x, ((0, 0), (K - 1, 0), (0, 0)))
    y = xp[:, 0:S] * w[0]
    for j in range(1, K):
        y = y + xp[:, j:j + S] * w[j]
    return y

def short_conv_mixer(hx, b, c, conv_w, norm_g):
    Bsz, S, _ = hx.shape
    y = b * causal_dwconv(c * hx, conv_w)
    y = y.reshape(Bsz, S, CONV_A_GROUPS, CONV_A_GROUP_DIM)
    y = rms_norm(y, norm_g.reshape(CONV_A_GROUPS, CONV_A_GROUP_DIM))
    return y.reshape(Bsz, S, CONV_A_DIM)

def chunk_gated_delta(q, k, v, beta, g):
    Bsz, H, S, dk = q.shape
    dv = v.shape[-1]
    n = S // CHUNK

    def chunks(t):
        return t.reshape((Bsz, H, n, CHUNK) + t.shape[3:])

    q, k, v, beta, g = chunks(q), chunks(k), chunks(v), chunks(beta), chunks(g)
    g = jnp.cumsum(g, axis=-1)
    causal = jnp.tril(jnp.ones((CHUNK, CHUNK), bool))
    strict = jnp.tril(jnp.ones((CHUNK, CHUNK), bool), -1)
    decay = jnp.exp(jnp.where(causal, g[..., :, None] - g[..., None, :], -jnp.inf))
    k_beta = k * beta[..., None]
    L = jnp.where(strict, jnp.einsum('bhncd,bhnjd->bhncj', k_beta, k) * decay, 0.0)
    eye = jnp.eye(CHUNK, dtype=jnp.float32)
    rhs = jnp.concatenate([v * beta[..., None], k_beta * jnp.exp(g)[..., None]], axis=-1)
    uw = lax.linalg.triangular_solve(eye + L, rhs, left_side=True, lower=True, unit_diagonal=True)
    u, w = uw[..., :dv], uw[..., dv:]
    intra = jnp.einsum('bhncd,bhnjd->bhncj', q, k) * decay
    q_dec = q * jnp.exp(g)[..., None]
    g_last = g[..., -1]
    k_dec = k * jnp.exp(g_last[..., None] - g)[..., None]

    def to_scan(t):
        return jnp.moveaxis(t, 2, 0)

    xs = (to_scan(u), to_scan(w), to_scan(q_dec), to_scan(intra), to_scan(k_dec), to_scan(g_last))

    def step(state, inp):
        u_i, w_i, qd_i, a_i, kd_i, gl_i = inp
        v_new = u_i - jnp.einsum('bhck,bhkv->bhcv', w_i, state)
        o_i = jnp.einsum('bhck,bhkv->bhcv', qd_i, state) + jnp.einsum('bhcj,bhjv->bhcv', a_i, v_new)
        state = state * jnp.exp(gl_i)[..., None, None] + jnp.einsum('bhck,bhcv->bhkv', kd_i, v_new)
        return state, o_i

    s0 = jnp.zeros((Bsz, H, dk, dv), jnp.float32)
    _, o = lax.scan(step, s0, xs)
    return jnp.moveaxis(o, 0, 2).reshape(Bsz, H, S, dv)

def gated_deltanet(q, k, v, z, beta_logit, a_logit, conv_w, a_log, dt_bias, norm_g):
    Bsz, S, _ = q.shape
    dtype = q.dtype
    qkv = jax.nn.silu(causal_dwconv(jnp.concatenate([q, k, v], axis=-1), conv_w)).astype(jnp.float32)
    q, k, v = jnp.split(qkv, 3, axis=-1)

    def heads(t):
        return t.reshape(Bsz, S, DN_HEADS, DN_HEAD_DIM).transpose(0, 2, 1, 3)

    q, k, v = heads(q), heads(k), heads(v)
    q = q * lax.rsqrt(jnp.sum(q * q, axis=-1, keepdims=True) + EPS) * (DN_HEAD_DIM ** -0.5)
    k = k * lax.rsqrt(jnp.sum(k * k, axis=-1, keepdims=True) + EPS)
    beta = jax.nn.sigmoid(beta_logit.astype(jnp.float32)).transpose(0, 2, 1)
    g = (-jnp.exp(a_log.astype(jnp.float32))
         * jax.nn.softplus(a_logit.astype(jnp.float32) + dt_bias.astype(jnp.float32))).transpose(0, 2, 1)
    o = chunk_gated_delta(q, k, v, beta, g).transpose(0, 2, 1, 3)
    zf = z.astype(jnp.float32).reshape(Bsz, S, DN_HEADS, DN_HEAD_DIM)
    o = rms_norm(o, norm_g) * jax.nn.silu(zf)
    return o.reshape(Bsz, S, DN_DIM).astype(dtype)

def hier_moe(h, router_group_w, router_expert_w, w_gate, w_up, w_down):
    N, D = h.shape
    group_logits = (h @ router_group_w).astype(jnp.float32)
    group_idx = jnp.argmax(group_logits, axis=-1)
    group_prob = jnp.take_along_axis(jax.nn.softmax(group_logits, axis=-1), group_idx[:, None], axis=1)
    exp_logits = (h @ router_expert_w).astype(jnp.float32).reshape(N, N_GROUPS, EXPERTS_PER_GROUP)
    exp_logits = jnp.take_along_axis(exp_logits, group_idx[:, None, None], axis=1)[:, 0]
    top_p, top_local = lax.top_k(jax.nn.softmax(exp_logits, axis=-1), TOP_K)
    gate = group_prob * top_p / jnp.sum(top_p, axis=-1, keepdims=True)
    expert_id = (group_idx[:, None] * EXPERTS_PER_GROUP + top_local).astype(jnp.int32)

    flat_e = expert_id.reshape(-1)
    flat_tok = jnp.repeat(jnp.arange(N, dtype=jnp.int32), TOP_K)
    flat_gate = gate.reshape(-1)
    order = jnp.argsort(flat_e)
    sorted_e = flat_e[order]
    counts = jnp.bincount(flat_e, length=N_EXPERTS)
    padded = (counts + MOE_BLOCK - 1) // MOE_BLOCK * MOE_BLOCK
    pad_end = jnp.cumsum(padded)
    pad_start = pad_end - padded
    start = jnp.cumsum(counts) - counts
    dest = pad_start[sorted_e] + jnp.arange(N * TOP_K, dtype=jnp.int32) - start[sorted_e]
    P = N * TOP_K + N_EXPERTS * MOE_BLOCK
    slot_tok = jnp.full((P,), N, jnp.int32).at[dest].set(flat_tok[order])
    slot_gate = jnp.zeros((P,), jnp.float32).at[dest].set(flat_gate[order])
    n_blocks = P // MOE_BLOCK
    block_expert = jnp.minimum(
        jnp.searchsorted(pad_end, jnp.arange(n_blocks, dtype=jnp.int32) * MOE_BLOCK, side='right'),
        N_EXPERTS - 1)
    h_pad = jnp.concatenate([h, jnp.zeros((1, D), h.dtype)], axis=0)
    xb = h_pad[slot_tok].reshape(n_blocks, MOE_BLOCK, D)

    def expert_block(args):
        xblk, e = args
        a = xblk @ w_gate[e]
        b = xblk @ w_up[e]
        return (jax.nn.silu(a) * b) @ w_down[e]

    yb = lax.map(expert_block, (xb, block_expert)).reshape(P, D)
    out = jnp.zeros((N + 1, D), jnp.float32).at[slot_tok].add(yb.astype(jnp.float32) * slot_gate[:, None])
    return out[:N].astype(h.dtype)

def second_inputs(seed: int = 0) -> dict:
    key = jax.random.key(seed)
    ks = jax.random.split(key, 18)
    f32 = jnp.float32

    def normal(k, shape, scale):
        return jax.random.normal(k, shape, f32) * scale

    def gain(k, shape):
        return 1.0 + 0.05 * jax.random.normal(k, shape, f32)

    dt = jnp.exp(jax.random.uniform(ks[7], (DEPTH_2, DN_HEADS), f32, math.log(1e-3), math.log(1e-1)))
    return {
        "x": normal(ks[0], (BATCH, SEQ, D_MODEL), 1.0),
        "mix_norm_g": gain(ks[1], (DEPTH_2, D_MODEL)),
        "w_in": normal(ks[2], (DEPTH_2, D_MODEL, IN_PROJ_DIM), D_MODEL ** -0.5),
        "conv_a_w": normal(ks[3], (DEPTH_2, CONV_A_WIDTH, CONV_A_DIM), CONV_A_WIDTH ** -0.5),
        "conv_a_norm_g": gain(ks[4], (DEPTH_2, CONV_A_DIM)),
        "dn_conv_w": normal(ks[5], (DEPTH_2, DN_CONV_WIDTH, 3 * DN_DIM), DN_CONV_WIDTH ** -0.5),
        "dn_a_log": jnp.log(jax.random.uniform(ks[6], (DEPTH_2, DN_HEADS), f32, 1.0, 16.0)),
        "dn_dt_bias": dt + jnp.log(-jnp.expm1(-dt)),
        "dn_norm_g": gain(ks[8], (DEPTH_2, DN_HEAD_DIM)),
        "w_out": normal(ks[9], (DEPTH_2, MIX_DIM, D_MODEL), MIX_DIM ** -0.5),
        "ffn_norm_g": gain(ks[10], (DEPTH_2, D_MODEL)),
        "router_group_w": normal(ks[11], (DEPTH_2, D_MODEL, N_GROUPS), D_MODEL ** -0.5),
        "router_expert_w": normal(ks[12], (DEPTH_2, D_MODEL, N_EXPERTS), D_MODEL ** -0.5),
        "w_gate": normal(ks[13], (DEPTH_2, N_EXPERTS, D_MODEL, EXPERT_FF), D_MODEL ** -0.5),
        "w_up": normal(ks[14], (DEPTH_2, N_EXPERTS, D_MODEL, EXPERT_FF), D_MODEL ** -0.5),
        "w_down": normal(ks[15], (DEPTH_2, N_EXPERTS, EXPERT_FF, D_MODEL), EXPERT_FF ** -0.5),
        "final_norm_g": gain(ks[16], (D_MODEL,)),
    }

def second_block(x, mix_norm_g, w_in, conv_a_w, conv_a_norm_g, dn_conv_w, dn_a_log, dn_dt_bias,
              dn_norm_g, w_out, ffn_norm_g, router_group_w, router_expert_w, w_gate, w_up, w_down,
              final_norm_g):
    Bsz, S, D = x.shape
    sizes = (CONV_A_DIM,) * 3 + (DN_DIM,) * 4 + (DN_HEADS,) * 2
    split_idx = []
    acc = 0
    for s in sizes[:-1]:
        acc += s
        split_idx.append(acc)
    for l in range(DEPTH_2):
        h = rms_norm(x, mix_norm_g[l])
        proj = h @ w_in[l]
        a_h, a_b, a_c, d_q, d_k, d_v, d_z, d_beta, d_alpha = jnp.split(proj, split_idx, axis=-1)
        y_a = short_conv_mixer(a_h, a_b, a_c, conv_a_w[l], conv_a_norm_g[l])
        y_b = gated_deltanet(d_q, d_k, d_v, d_z, d_beta, d_alpha, dn_conv_w[l], dn_a_log[l],
                             dn_dt_bias[l], dn_norm_g[l])
        x = x + jnp.concatenate([y_a, y_b], axis=-1) @ w_out[l]
        h = rms_norm(x, ffn_norm_g[l]).reshape(Bsz * S, D)
        x = x + hier_moe(h, router_group_w[l], router_expert_w[l], w_gate[l], w_up[l], w_down[l]).reshape(Bsz, S, D)
    return rms_norm(x, final_norm_g)


def setup_inputs(seed=0):
    out = dict(first_inputs(seed))
    for name, value in second_inputs(seed + 1).items():
        if name != "x":
            out[name + "_2"] = value
    return out


def reference(
    x, mem, norm_g, fox_w_in, fox_b_f, ret_w_in, mem_norm_g, w_mem_kv, w_out, final_norm_g,
    mix_norm_g_2, w_in_2, conv_a_w_2, conv_a_norm_g_2, dn_conv_w_2, dn_a_log_2, dn_dt_bias_2,
    dn_norm_g_2, w_out_2, ffn_norm_g_2, router_group_w_2, router_expert_w_2, w_gate_2, w_up_2,
    w_down_2, final_norm_g_2,
):
    x = first_block(
        x, mem, norm_g, fox_w_in, fox_b_f, ret_w_in, mem_norm_g, w_mem_kv, w_out, final_norm_g,
    )
    return second_block(
        x, mix_norm_g_2, w_in_2, conv_a_w_2, conv_a_norm_g_2, dn_conv_w_2, dn_a_log_2,
        dn_dt_bias_2, dn_norm_g_2, w_out_2, ffn_norm_g_2, router_group_w_2, router_expert_w_2,
        w_gate_2, w_up_2, w_down_2, final_norm_g_2,
    )


_drawn_inputs = setup_inputs


def setup_inputs(seed=0):
    import zlib

    import numpy as np

    out = dict(_drawn_inputs(seed))
    spreads = {}
    factors = {'mem_norm_g': 6.966}
    for name, (base, spread) in spreads.items():
        noise = np.random.default_rng([zlib.crc32(name.encode()), seed]).standard_normal(out[name].shape)
        drawn = base * np.exp(spread * noise) if base else spread * noise
        out[name] = __import__('jax').numpy.asarray(drawn.astype(out[name].dtype))
    for name, factor in factors.items():
        out[name] = (out[name] * factor).astype(out[name].dtype)
    return out
```

```python
import concourse.bass as bass
from concourse import mybir
from contextlib import ExitStack

F32 = mybir.dt.float32
F32R = mybir.dt.float32r
I32 = mybir.dt.int32
ALU = mybir.AluOpType
ACT = mybir.ActivationFunctionType
AX = mybir.AxisListType

P = 128
S = 512
D = 1024
NT = S // P
KD = D // P
NM = 256
HD = 128
NMAIN, NMEM = 12, 4
MAIN_W, MEM_W = NMAIN * HD, NMEM * HD
INNER = MAIN_W + MEM_W
NEG = -1e30
EPS = 1e-6
QK_SCALE = float(HD) ** -0.5
RET_SCALE = float(HD // 2) ** -0.5

C_ID, C_ONE, C_TRI, C_STRI, C_CM, C_CMT, C_PERM, C_BD, C_LVL = [P * n for n in range(9)]
NLVL = 7
C_END = C_LVL + NLVL * P
V_DNCONV, V_ACONV, V_ANORM, V_DNNORM, V_END = 0, 48, 60, 64, 65
N_F, N_BA, N_R, N_END = 0, 12, 20, 56

PANEL = 2048
RAW, SPLIT = 2, 3

NG, EPG = 4, 8
NE = NG * EPG
FF = 512
CAP = 64
NOV = (2 * S - 1) // CAP
NB = NE + NOV + 1
MRAW = 6
R_W4, R_W8, R_I32, R_J, R_END = 0, 4, 12, 12, 44


def make_schedule():
    panels, steps, units = [], [], []

    def panel(kind, n, **meta):
        panels.append(dict(kind=kind, n=n, first=len(steps), **meta))
        for c in range(n):
            steps.append(dict(kind=kind, c=c, n=n, panel=len(panels) - 1, slots=[], **meta))

    for layer in range(2):
        for half in range(2):
            panel("kmT", 2, layer=layer, half=half)
        for half in range(2):
            panel("vm", 2, layer=layer, half=half)
        u0 = len(units)
        for g in range(8):
            mem = g < 2
            for h in range(2):
                for i in range(NT):
                    kind = "mem" if mem else ("fox", "ret")[layer]
                    w = NM if mem else ((i + 1) * P if layer == 0 else (NT - i) * P)
                    units.append(dict(kind=kind, layer=layer, g=g, h=h, i=i, w=w, mem=mem,
                                      head=16 * layer + 2 * g + h))
        def project(g):
            first = len(steps)
            if g < 2:
                panel("q", 2, layer=layer, g=g)
            elif layer == 0:
                panel("q", 2, layer=layer, g=g)
                panel("k", 2, layer=layer, g=g)
                panel("v", 2, layer=layer, g=g)
            else:
                panel("rqk", 2, layer=layer, g=g)
                panel("v", 2, layer=layer, g=g)
            panel("z", 2, layer=layer, g=g)
            return steps[first:]

        def attach(slots, into):
            for j, k in enumerate(slots):
                into[j * len(into) // len(slots)]["slots"].append(k)

        for g in range(8):
            new = project(g)
            if g == 0:
                attach(range(u0, u0 + 2), new[2:])
            elif g == 1:
                attach(range(u0 + 2, u0 + 10), new)
            else:
                attach(range(u0 + 8 * g - 6, u0 + 8 * g), new)
            if g >= 2 and g < 7:
                first = len(steps)
                panel("o", 4, layer=layer, g=g - 2)
                attach(range(u0 + 8 * g, u0 + 8 * g + 2), steps[first:])
        first = len(steps)
        panel("o", 4, layer=layer, g=5)
        panel("o", 4, layer=layer, g=6)
        attach(range(u0 + 56, u0 + 64), steps[first:])
        steps[-1]["slots"] += [u0 + 64, u0 + 65, u0 + 66]
        panel("o", 4, layer=layer, g=7)
    for kind in ("cq", "ck", "cv", "gz"):
        for half in range(2):
            panel(kind, 2, layer=2, half=half)
    for half in range(2):
        for kind in ("ah", "ac", "ab"):
            panel(kind, 2, layer=2, half=half)
    for g in range(4):
        panel("o2", 4, layer=2, g=g)
    return panels, steps, units


def program(nc, A, out, debug):
    panels, steps, units = make_schedule()
    NSTEP, NPANEL, NUNIT = len(steps), len(panels), len(units)

    count = {"act": 0, "dve": 0}
    for st in steps:
        who = "dve" if st["kind"] in ("z", "o", "o2", "rqk", "gz", "ac", "ab") else "act"
        count[who] += 1
        st["freed"] = (who, count[who])
    pieces = []
    for pn in panels:
        pieces.append((pieces[-1] if pieces else 0) + pn["n"])
    nsoft, nret = 0, 0
    for un in units:
        un["soft"] = nsoft
        un["ret"] = nret
        if un["kind"] != "ret":
            nsoft += 1
        elif un["i"] == NT - 1:
            nret += 1
    def last_unit(layer, g):
        return 64 * layer + 8 * g + 7

    def panel_end(n):
        return panels[n]["first"] + panels[n]["n"]

    z_freed = [st["freed"][1] for st in steps if st["kind"] in ("z", "gz")]
    rope_steps = [s for s, st in enumerate(steps) if st["kind"] == "rqk"]

    def rope_no(s):
        return rope_steps.index(s)

    def nsoft_of(layer):
        return sum(un["kind"] != "ret" for un in units if un["layer"] <= layer)

    def in_layer(k, layer):
        return 0 <= k - 64 * layer < 64

    layer_first = [min(i for i, st in enumerate(steps) if st["layer"] == l) for l in range(3)]
    first_step = [min(i for i, st in enumerate(steps) if st["layer"] == l and st["kind"] == "q") for l in range(2)]
    conv_steps = [s for s, st in enumerate(steps) if st["kind"] in ("cq", "ck", "cv")]
    norm_steps = [s for s, st in enumerate(steps) if st["kind"] in ("cq", "ck", "ab")]
    a_steps = [s for s, st in enumerate(steps) if st["kind"] == "ac"]
    o2_first = min(s for s, st in enumerate(steps) if st["kind"] == "o2")
    gdn_step = o2_first + 8
    o_panel = {(pn["layer"], pn["g"]): n for n, pn in enumerate(panels) if pn["kind"] == "o"}
    last_kv_step = [max(i for i, st in enumerate(steps) if st["layer"] == l and st["kind"] == "vm") for l in range(2)]
    tz_before, n_z = [], 0
    for st in steps:
        tz_before.append(n_z)
        n_z += st["kind"] in ("z", "gz")

    with ExitStack() as ctx:
        top = [16512]

        def at(name, shape, dt=F32, offset=None):
            size = 4
            for n in shape[1:]:
                size *= n
            if offset is None:
                offset = top[0]
                top[0] += (size + 31) // 32 * 32
            t = nc.alloc_sbuf_tensor_at(name, shape, dt, offset=offset)
            return t, offset

        cst, _ = at("cst", [P, C_END])
        x, _ = at("x", [P, NT, D])
        gbc, o_gbc = at("gbc", [P, D])
        rope, _ = at("rope", [P, 2, S], offset=o_gbc)
        wn_raw, _ = at("wn_raw", [P, KD, N_END])
        wn_hi, _ = at("wn_hi", [P, KD, N_END], F32R)
        wn_lo, _ = at("wn_lo", [P, KD, N_END], F32R)
        st_, _ = at("stats", [P, 256])
        w_hi, _ = at("w_hi", [P, SPLIT, PANEL], F32R)
        w_lo, _ = at("w_lo", [P, SPLIT, PANEL], F32R)
        w_raw, _ = at("w_raw", [P, RAW, PANEL])
        hT_hi, o_hT = at("hT_hi", [P, KD, S], F32R)
        hT_lo, _ = at("hT_lo", [P, KD, S], F32R)
        aux, o_aux = at("aux", [P, 2, 2, S])
        qT, o_q = at("qT", [P, 2, 2, S])
        kT, _ = at("kT", [P, 2, 2, S])
        v, _ = at("v", [P, 2, NT, 256])
        mT_hi, _ = at("mT_hi", [P, KD, NM], F32R, offset=o_q)
        mT_lo, _ = at("mT_lo", [P, KD, NM], F32R, offset=o_q + 4 * KD * NM)
        zs, _ = at("zs", [P, 2, 2, S])
        oT_hi, _ = at("oT_hi", [P, 2, 2, S], F32R)
        oT_lo, _ = at("oT_lo", [P, 2, 2, S], F32R)
        kmT, _ = at("kmT", [P, NMEM, NM])
        vm, _ = at("vm", [P, 2, MEM_W])
        sc, o_s = at("sc", [P, 2, S])
        pT, _ = at("pT", [P, 2, S])
        og, _ = at("og", [P, S])
        tz, _ = at("tz", [P, S])
        assert top[0] + 2048 <= nc.sbuf_usable_end
        negc, _ = at("negc", [NMAIN, S], offset=top[0])
        xn, _ = at("xn", [P, 2, D], offset=o_s)
        sq, o_sq = at("sq", [P, S], offset=o_s + 4096)
        rt, _ = at("rt", [P, S], offset=top[0])
        gbr = aux[:].rearrange("p a b s -> p (a b) s")
        gq, _ = at("gq", [P, 4, S], offset=o_q)
        gk, _ = at("gk", [P, 4, S], offset=o_q + 8192)
        gv, _ = at("gv", [P, 4, S], offset=o_q + 16384)
        gz, _ = at("gz", [P, 4, S], offset=o_q + 24576)
        ya_hi, _ = at("ya_hi", [P, 4, S], F32R, offset=o_q + 32768)
        ya_lo, _ = at("ya_lo", [P, 4, S], F32R, offset=o_q + 40960)
        o_f = o_q + 49152
        hb, _ = at("hb", [P, 2, S], offset=o_f)
        sg, _ = at("sg", [P, 2, 520], offset=o_f + 4096)
        tz2, _ = at("tz2", [P, S], offset=o_f + 8256)
        sq2, _ = at("sq2", [P, 2, S], offset=o_f + 10304)
        gT, _ = at("gT", [4, S], offset=o_f)
        vn, _ = at("vn", [P, 4, S], offset=o_f)
        kg, _ = at("kg", [P, 4, S], offset=o_f + 8192)
        kd = gv
        dt_, _ = at("dt", [P, S], offset=o_f + 16384)
        dT, _ = at("dT", [P, S], offset=o_f + 18432)
        bt, _ = at("bt", [P, 2, S], offset=o_gbc)
        gs, _ = at("gs", [P, 512], offset=top[0])
        nT, _ = at("nT", [36, S], offset=top[0])
        T_, _ = at("T", [P, 4, S], offset=o_hT)
        TT, _ = at("TT", [P, 4, S], offset=o_hT + 8192)
        U, _ = at("U", [P, 4, S], offset=o_hT + 16384)
        LT, _ = at("LT", [P, 4, S], offset=o_hT + 24576)
        nw, iT, ob = T_, LT, gk
        SS, _ = at("SS", [P, 2, S], offset=o_hT + 16384)
        vnw, _ = at("vnw", [P, 2, S], offset=o_hT + 16384 + 4096)
        yb_hi, _ = at("yb_hi", [P, 4, S], F32R, offset=o_hT)
        yb_lo, _ = at("yb_lo", [P, 4, S], F32R, offset=o_hT + 8192)
        vecs = st_[:, 140:140 + V_END]
        rowc = st_[:, 205:205 + R_END]
        m_raw, _ = at("m_raw", [P, MRAW, PANEL], offset=o_aux)
        o_m = o_aux + 4 * MRAW * PANEL
        xs, _ = at("xs", [P, D], offset=o_m)
        xT_hi, _ = at("xT_hi", [P, KD, CAP], F32R, offset=o_m + 4096)
        xT_lo, _ = at("xT_lo", [P, KD, CAP], F32R, offset=o_m + 8192)
        ys, _ = at("ys", [P, D], offset=o_m + 12288)
        mtz, _ = at("mtz", [P, FF], offset=o_hT)
        msl, _ = at("msl", [P, FF], offset=o_hT + 2048)
        mid, _ = at("mid", [P, FF], offset=o_hT + 4096)
        mT_h, _ = at("mT_h", [P, 4, CAP], F32R, offset=o_hT + 6144)
        mT_l, _ = at("mT_l", [P, 4, CAP], F32R, offset=o_hT + 8192)
        yg, _ = at("yg", [P, 2 * NT, D], offset=o_aux)
        rb, _ = at("rb", [P, 2048], offset=o_hT + 18432)
        oi = 16512 + 4 * C_END + 4 * NT * D + 4 * D
        ti, _ = at("ti", [P, NT], I32, offset=oi)
        di, _ = at("di", [P, 8], I32, offset=oi + 32)
        yi, _ = at("yi", [P, 8], I32, offset=oi + 64)
        ix, _ = at("ix", [P, NB], I32, offset=oi + 96)
        ov, _ = at("ov", [P, NOV + 1], I32, offset=oi + 96 + 4 * NB)
        fld, c0 = {}, 0
        for name, n in (("L", 36), ("gs", 4), ("ge", 4), ("gw", 4), ("goh", 4), ("t4", 32), ("sel", 8), ("w8", 8),
                        ("oh0", 8), ("oh1", 8), ("E0", 32), ("E1", 32), ("E", 32), ("tm", 32)):
            fld[name] = rb[:, c0:c0 + NT * n].rearrange("p (t n) -> p t n", t=NT)
            c0 += NT * n
        def col(n):
            nonlocal c0
            c0 += n
            return rb[:, c0 - n:c0]
        gmx, gpm, m0, m1, gp, de, gsum = [col(4) for _ in range(7)]
        rk, ovk, ek, qk_, blk, tq = [col(8) for _ in range(6)]
        cnt, ovc, ovi, ove = [col(32) for _ in range(4)]
        cmp7 = col(NOV * NE)
        cx = col(NOV + 1)
        assert c0 <= 2048
        gates = gs[:, 224:232]
        ba = gs[:, 0:32].rearrange("p (c n) -> p c n", c=4)
        bexp, aexp, aabs = gs[:, 32:48], gs[:, 48:64], gs[:, 64:80]
        beta, lg, gn, egn, gl, edk, egl = [gs[:, 80 + 16 * n:96 + 16 * n] for n in range(7)]
        nea = gs[:, 192:196]
        ngn = gs[:, 196:212]
        logf = st_[:, 0:48]
        absf = st_[:, 48:96]
        fb = st_[:, 96:116]
        mx = st_[:, 116:118]
        rs = st_[:, 118:120]
        ss = st_[:, 120:124]
        rstd = st_[:, 124:128]
        epst = st_[:, 128:129]
        rsum = st_[:, 130:132]
        rinv = st_[:, 132:134]
        sd = st_[:, 134:138]

        PJ = [ctx.enter_context(nc.psum_tensor(f"PJ{i}", [P, D], F32)) for i in range(2)]
        PB = [ctx.enter_context(nc.psum_tensor(f"PB{i}", [P, S], F32)) for i in range(4)]
        PS, PT, PO = PB[0:2], PB[2], PB[3]

        def sem(name):
            return ctx.enter_context(nc.semaphore(name))

        s_cst, s_x = sem("s_cst"), sem("s_x")
        s_const = sem("s_const")
        s_mem = sem("s_mem")
        s_gain = sem("s_gain")
        raw_full = [sem(f"raw_full{i}") for i in range(RAW)]
        hi_done = sem("hi_done")
        lo_done = sem("lo_done")
        mm_done = sem("mm_done")
        freed_act = sem("freed_act")
        freed_dve = sem("freed_dve")
        freed = {"act": freed_act, "dve": freed_dve}
        tz_ready = sem("tz_ready")
        s_wn = sem("s_wn")
        s_eps = sem("s_eps")
        n_ss = sem("n_ss")
        n_ms = sem("n_ms")
        n_sd = sem("n_sd")
        n_xn = sem("n_xn")
        n_tr = sem("n_tr")
        n_hi = sem("n_hi")
        n_lo = sem("n_lo")
        f_mm = sem("f_mm")
        f_in = sem("f_in")
        f_ab = sem("f_ab")
        f_ln = sem("f_ln")
        f_log = sem("f_log")
        f_cum = sem("f_cum")
        f_neg = sem("f_neg")
        f_dram = sem("f_dram")
        aux_full = [sem(f"aux_full{i}") for i in range(2)]
        s_ready = sem("s_ready")
        s_read = sem("s_read")
        m_ready = sem("m_ready")
        e_done = sem("e_done")
        p_ready = sem("p_ready")
        t_done = sem("t_done")
        t_copied = sem("t_copied")
        v_done = sem("v_done")
        o_dve = sem("o_dve")
        o_act = sem("o_act")
        ms_done = sem("ms_done")
        sd_done = sem("sd_done")
        og_used = sem("og_used")
        ot_done = sem("ot_done")
        rr_ready = sem("rr_ready")
        perm_done = sem("perm_done")
        d_mm = sem("d_mm")
        d_in, d_act, d_gate, d_cum, d_gn, d_gT, d_dram, d_gb, d_e, d_e2 = [
            sem(n) for n in ("d_in", "d_act", "d_gate", "d_cum", "d_gn", "d_gT", "d_dram", "d_gb", "d_e", "d_e2")]
        cv_done = sem("cv_done")
        tz_ready2 = sem("tz_ready2")
        si_done = sem("si_done")
        q_ready = sem("q_ready")
        q_sum = sem("q_sum")
        q_sd = sem("q_sd")
        q_fin = sem("q_fin")
        a_h = sem("a_h")
        s_pad = sem("s_pad")
        g_tr, g_vn, g_kg, g_D, g_dT, g_kk, g_LT, g_bt, g_umm, g_uc, g_tmm, g_tup = [
            sem(n) for n in ("g_tr", "g_vn", "g_kg", "g_D", "g_dT", "g_kk", "g_LT", "g_bt", "g_umm", "g_uc", "g_tmm",
                             "g_tup")]
        g_nmm, g_nw, g_imm, g_iT, g_eg, g_qd, g_vmm, g_vne, g_omm, g_oe, g_smm, g_se = [
            sem(n) for n in ("g_nmm", "g_nw", "g_imm", "g_iT", "g_eg", "g_qd", "g_vmm", "g_vne", "g_omm", "g_oe",
                             "g_smm", "g_se")]
        y_sq, y_ms, y_sd, y_fin = [sem(n) for n in ("y_sq", "y_ms", "y_sd", "y_fin")]
        nr_mm, nr_sb = sem("nr_mm"), sem("nr_sb")
        y_zero = sem("y_zero")
        m_full = [sem(f"m_full{i}") for i in range(MRAW)]
        hn_st = [sem("hn_st0"), sem("hn_st1")]
        (r_mm, r_g, r_e, r_E, r_rk, r_d, r_dst, r_ov, r_tab, r_sc, r_ix, r_set) = [
            sem(n) for n in ("r_mm", "r_g", "r_e", "r_E", "r_rk", "r_d", "r_dst", "r_ov", "r_tab", "r_sc",
                             "r_ix", "r_set")]
        m_hi, m_lo, m_mm, x_g, x_tr, x_hi, x_lo = [
            sem(n) for n in ("m_hi", "m_lo", "m_mm", "x_g", "x_tr", "x_hi", "x_lo")]
        h_th, h_mid, h_tr, h_hi, h_lo, y_ev, y_st = [
            sem(n) for n in ("h_th", "h_mid", "h_tr", "h_hi", "h_lo", "y_ev", "y_st")]
        o_full = [sem(f"o_full{i}") for i in range(MRAW)]
        o_hi, o_lo, o_mm = [sem(n) for n in ("o_hi", "o_lo", "o_mm")]
        c_g = [sem(f"c_g{i}") for i in range(2 * NT)]
        h_sl = sem("h_sl")
        c_x = sem("c_x")
        s_out = sem("s_out")
        s_x1 = sem("s_x1")
        s_dbg = sem("s_dbg")
        a_ch = sem("a_ch")
        v_ch = sem("v_ch")

        ident = cst[:, C_ID:C_ID + P]

        def mm3(pe, dst, lhs, rhs, start, stop):
            (lh, ll), (rh, rl) = lhs, rhs
            pe.matmul(dst, lh, rh, start=start, stop=False)
            pe.matmul(dst, lh, rl, start=False, stop=False)
            return pe.matmul(dst, ll, rh, start=False, stop=stop)

        def w_view(n, k):
            sl = n % SPLIT
            return tuple(t[:, sl, :].rearrange("p (k n) -> p k n", k=k) for t in (w_hi, w_lo))

        def gain_wait(eng, n):
            eng.wait_ge(s_gain, 16 * n)

        NORMS = [("mem", 2), ("x", 4), ("mem", 2), ("x", 4), ("self", 0), ("x", 4), ("x", 4),
                 ("self", 0)]
        tiles_before = [0, 2, 6, 8, 12, 12, 16, 20]
        gains_before = [1, 2, 3, 4, 6, 7, 8, 9]
        dve_freed_layer = [max(st["freed"][1] for st in steps if st["layer"] == l and st["freed"][0] == "dve")
                           for l in range(3)]

        block = ctx.enter_context(nc.Block())

        @block.sync
        def _(sp):
            sp.dma_start(cst[:], A["cst"]).then_inc(s_cst, 16)
            sp.dma_start(x[:], A["x"].rearrange("(t p) d -> p t d", p=P)).then_inc(s_x, 16)
            for n, pn in enumerate(panels):
                if n == 1:
                    sp.dma_start(wn_raw[:], A["wn"].rearrange("(k p) n -> p k n", p=P)).then_inc(s_const, 16)
                    sp.dma_start(fb, A["rows"].broadcast_to([P, 20])).then_inc(s_const, 16)
                    sp.dma_start(vecs, A["vecs"]).then_inc(s_const, 16)
                    sp.dma_start(rowc, A["rowc"].broadcast_to([P, R_END])).then_inc(s_const, 16)
                if n >= RAW:
                    sp.wait_ge(hi_done, pieces[n - RAW])
                    sp.wait_ge(lo_done, pieces[n - RAW])
                L, kind = pn["layer"], pn["kind"]
                dst = w_raw[:, n % RAW, :]
                if kind in ("o", "o2"):
                    g = pn["g"]
                    if kind == "o":
                        r0 = MAIN_W + 256 * g if g < 2 else 256 * (g - 2)
                        src = A["w_out"][L, r0:r0 + 256, :].rearrange("(k p) n -> p k n", p=P)
                    else:
                        src = A["w_out_2"][256 * g:256 * g + 256, :].rearrange("(k p) n -> p k n", p=P)
                    sp.dma_start(dst.rearrange("p (k n) -> p k n", k=2), src).then_inc(raw_full[n % RAW], 16)
                    continue
                if kind == "kmT" or kind == "vm":
                    c0 = 256 * pn["half"] + (MEM_W if kind == "vm" else 0)
                    w = A["w_mem_kv"][L]
                    cols = [c0]
                elif L == 2:
                    w = A["w_in_2"]
                    cols = [S * ("ah", "ab", "ac", "cq", "ck", "cv", "gz").index(kind) + 256 * pn["half"]]
                else:
                    g = pn["g"]
                    w = A["fox_w_in"] if L == 0 else A["ret_w_in"]
                    zc = 3 * MAIN_W + NMAIN + MEM_W if L == 0 else 2 * MAIN_W + MEM_W
                    zc += MAIN_W + 256 * g if g < 2 else 256 * (g - 2)
                    qm = (3 * MAIN_W + NMAIN if L == 0 else 2 * MAIN_W) + 256 * g
                    m = 256 * (g - 2)
                    if kind == "z":
                        cols = [zc]
                    elif g < 2:
                        cols = [qm]
                    elif L == 0:
                        cols = [{"q": 0, "k": MAIN_W, "v": 2 * MAIN_W}[kind] + m]
                    elif kind == "v":
                        cols = [MAIN_W + m]
                    else:
                        cols = [m // 2, MAIN_W // 2 + m // 2]
                k3 = dst.rearrange("p (k n) -> p k n", k=KD)
                wd = 256 // len(cols)
                for j, c0 in enumerate(cols):
                    src = w[:, c0:c0 + wd].rearrange("(k p) n -> p k n", p=P)
                    sp.dma_start(k3[:, :, j * wd:(j + 1) * wd], src).then_inc(raw_full[n % RAW], 16)
            def load_panel(e, j, slot, full):
                dst = m_raw[:, slot, :]
                hf = j % 2
                one = slice(e, e + 1) if isinstance(e, int) else bass.ds(e, 1)
                if j < 4:
                    w = A[("w_gate", "w_up")[j // 2]][one, 512 * hf:512 * hf + 512, :]
                    k = 4
                else:
                    w = A["w_down"][one, 256 * hf:256 * hf + 256, :]
                    k = 2
                sp.dma_start(dst.rearrange("p (k n) -> p k n", k=k),
                             w.rearrange("o (k p) n -> p (o k) n", p=P)).then_inc(full[slot], 16)

            sp.wait_ge(y_fin, 4)
            sp.wait_ge(mm_done, gdn_step)
            for j in range(4):
                load_panel(0, j, j, m_full)
            for j in range(6):
                n = 4 + j
                if n >= MRAW:
                    sp.wait_ge(m_lo, n - MRAW + 1)
                load_panel(1 if j < 4 else 0, j, n % MRAW, m_full)
            with sp.Fori(2, NE) as e:
                for j in range(6):
                    sp.wait_ge(m_lo, e * 6 + (4 + j - 6 - MRAW + 1))
                    load_panel(e if j < 4 else e - 1, j, (4 + j) % MRAW, m_full)
            for j in range(2):
                sp.wait_ge(m_lo, 6 * NE + 4 + j - 6 - MRAW + 1)
                load_panel(NE - 1, 4 + j, (4 + j) % MRAW, m_full)
            sp.wait_ge(r_ov, 1)
            with sp.register("sp_nov") as r:
                sp.reg_load(r, ov[0:1, NOV:NOV + 1])
                with sp.If(sp.snap(r) > 0):
                    sp.wait_ge(m_lo, 6 * NE)
                    for b in range(NOV):
                        with sp.register(f"sp_e{b}") as re:
                            sp.reg_load(re, ov[0:1, b:b + 1])
                            e = nc.s_assert_within(sp.snap(re), 0, NE - 1)
                            for j in range(6):
                                if b:
                                    sp.wait_ge(o_lo, 6 * (b - 1) + j + 1)
                                load_panel(e, j, j, o_full)
            for t in range(NT):
                sp.wait_ge(s_x1, 5 + t)
                sp.dma_start(out[0, t * P:(t + 1) * P, :], x[:, t, :]).then_inc(s_out, 16)
            sp.wait_ge(s_out, 64)

        raw_count, per_slot = [], [0] * RAW
        for n, pn in enumerate(panels):
            per_slot[n % RAW] += 32 if pn["kind"] == "rqk" else 16
            raw_count.append(per_slot[n % RAW])

        @block.gpsimd
        def _(pool):
            pool.dma_start(gbc[:], A["gains"][2:3, :].broadcast_to([P, D])).then_inc(s_gain, 16)
            for L in range(2):
                if L == 1:
                    pool.wait_ge(ot_done, 16)
                    pool.wait_ge(t_copied, nsoft_of(0))
                    pool.wait_ge(v_done, 64)
                    pool.wait_ge(tz_ready, tz_before[first_step[1]])
                    pool.wait_ge(n_xn, tiles_before[2])
                    pool.dma_start(gbc[:], A["gains"][2:3, :].broadcast_to([P, D])).then_inc(s_gain, 16)
                pool.dma_start(xn[:], A["mem"].rearrange("(t p) d -> p t d", p=P)).then_inc(s_mem, 16)
                pool.wait_ge(n_xn, tiles_before[2 * L + 1])
                pool.dma_start(gbc[:], A["gains"][L:L + 1, :].broadcast_to([P, D])).then_inc(s_gain, 16)
                if L == 0:
                    pool.wait_ge(f_neg, 1)
                    pool.dma_start(A["scr_c"], negc[:]).then_inc(f_dram, 16)
                    pool.wait_ge(f_dram, 16)
                else:
                    pool.wait_ge(n_xn, tiles_before[4])
                    pool.dma_start(rope[:], A["rope"].rearrange("a p s -> p a s")).then_inc(s_gain, 16)
                for g in range(2, 8):
                    if L or g >= 4:
                        pool.wait_ge(s_read, 64 * L + 8 * (g - 1) if g >= 4 else 64 * L)
                    m = 2 * (g - 2)
                    dst = aux[:, g % 2, :, :]
                    src = (A["scr_c"][m:m + 2, :].partition_broadcast(P) if L == 0
                           else A["decay"][:, m:m + 2, :])
                    pool.dma_start(dst, src).then_inc(aux_full[g % 2], 16)
            pool.wait_ge(freed_dve, dve_freed_layer[1])
            pool.dma_start(gbc[:], A["gains"][6:7, :].broadcast_to([P, D])).then_inc(s_gain, 16)
            pool.wait_ge(s_x1, 4)
            pool.dma_start(gbc[:], A["gains"][3:4, :].broadcast_to([P, D])).then_inc(s_gain, 16)
            pool.wait_ge(d_gT, 1)
            pool.dma_start(A["scr_g"], gT[:]).then_inc(d_dram, 16)
            pool.wait_ge(d_dram, 16)
            pool.dma_start(gbr, A["scr_g"].partition_broadcast(P)).then_inc(d_gb, 16)
            n = 0
            pool.wait_ge(n_xn, tiles_before[6])
            for l in range(NLVL):
                m = cst[:, C_LVL + l * P:C_LVL + (l + 1) * P].unsqueeze(1).broadcast_to([P, 4, P])
                for c in range(4):
                    pool.wait_ge(g_LT, c + 1)
                    if n >= 2:
                        pool.wait_ge(g_umm, n - 1)
                    pool.tensor_tensor(bt[:, n % 2, :].rearrange("p (h n) -> p h n", h=4),
                                       LT[:, c, :].rearrange("p (h n) -> p h n", h=4), m, ALU.mult).then_inc(g_bt, 1)
                    n += 1
            pool.wait_ge(g_umm, 4 * NLVL)
            pool.dma_start(gbc[:], A["gains"][4:5, :].broadcast_to([P, D])).then_inc(s_gain, 16)
            pool.iota(ti[:], [[P, NT]], base=0, channel_multiplier=1).then_inc(r_set, 1)
            pool.memset(ix[:], S).then_inc(r_set, 1)
            pool.wait_ge(r_set, 2)
            pool.dma_start(A["scr_tab"].rearrange("(p b) o -> p (b o)", p=CAP), ix[0:CAP, :]).then_inc(r_tab, 16)
            pool.wait_ge(y_fin, 4)
            pool.wait_ge(mm_done, gdn_step)
            pool.memset(xs[:], 0.0).then_inc(r_set, 1)
            pool.wait_ge(r_set, 3)
            for r0 in range(NE * CAP, (NE + NOV) * CAP, P):
                r1 = min(r0 + P, (NE + NOV) * CAP)
                pool.dma_start(A["scr_y"][r0:r1, :], xs[0:r1 - r0, :]).then_inc(y_zero, 16)
            for t in range(NT):
                pool.wait_ge(n_xn, tiles_before[6] + t + 1)
                pool.dma_start(A["scr_h"][t * P:(t + 1) * P, :], xn[:, t % 2, :]).then_inc(hn_st[t % 2], 16)
            pool.dma_start(gbc[:], A["gains"][5:6, :].broadcast_to([P, D])).then_inc(s_gain, 16)
            pool.wait_ge(r_tab, 16)
            pool.wait_ge(r_dst, 1)
            for n in range(8):
                pool.indirect_dma_start(A["scr_tab"], bass.IndirectOffsetOnAxis(ap=di[:, n:n + 1], axis=0),
                                        ti[:, n % 4:n % 4 + 1], None).then_inc(r_sc, 16)
            pool.wait_ge(r_sc, 128)
            pool.dma_start(ix[0:CAP, :], A["scr_tab"].rearrange("(p b) o -> p (b o)", p=CAP)).then_inc(r_ix, 16)
            pool.wait_ge(r_ix, 16)
            pool.wait_ge(y_zero, 16 * -(-NOV * CAP // P))
            pool.wait_ge(hn_st[0], 16 * NT // 2)
            pool.wait_ge(hn_st[1], 16 * NT // 2)

            def gather(b):
                if b:
                    pool.wait_ge(x_tr, b)
                    pool.wait_ge(x_g, 16 * b)
                pool.indirect_dma_start(xs[0:CAP, :], None, A["scr_h"],
                                        bass.IndirectOffsetOnAxis(ap=ix[0:CAP, b:b + 1], axis=0),
                                        bounds_check=S - 1, oob_is_err=False).then_inc(x_g, 16)

            for b in range(NE + 1):
                gather(b)
            with pool.register("pool_nov") as r:
                pool.reg_load(r, ov[0:1, NOV:NOV + 1])
                with pool.If(pool.snap(r) > 0):
                    for b in range(NE + 1, NB):
                        gather(b)
                    pool.wait_ge(y_st, 16 * (NE + NOV))
            pool.wait_ge(y_st, 16 * NE)
            for n in range(2 * NT):
                i = n % 2 * NT + n // 2
                pool.indirect_dma_start(yg[:, n, :], None, A["scr_y"],
                                        bass.IndirectOffsetOnAxis(ap=yi[:, i:i + 1], axis=0),
                                        bounds_check=(NE + NOV) * CAP - 1, oob_is_err=False).then_inc(c_g[n], 16)

        @block.scalar
        def _(act):
            ch = [0]

            def link(ins):
                ch[0] += 1
                ins.then_inc(a_ch, 1)
                act.wait_ge(a_ch, ch[0])

            def rsqrt(dst, src, scale):
                link(act.activation(dst, src, ACT.Ln, scale=scale, bias=epst))
                return act.activation(dst, dst, ACT.Exp, scale=-0.5)

            def split_hi(n, j):
                cnt = panels[n]["n"]
                w = PANEL // cnt
                if j == 0:
                    act.wait_ge(raw_full[n % RAW], raw_count[n])
                    if n >= SPLIT:
                        act.wait_ge(mm_done, panel_end(n - SPLIT))
                act.activation(w_hi[:, n % SPLIT, j * w:(j + 1) * w], w_raw[:, n % RAW, j * w:(j + 1) * w],
                               ACT.Copy).then_inc(hi_done, 1)

            def norm_squares(n):
                kind, nt = NORMS[n]
                if kind == "mem":
                    act.wait_ge(s_mem, 16 * (n // 2 + 1))
                if n == 1:
                    act.wait_ge(s_x, 16)
                if n == 5:
                    act.wait_ge(s_x1, 4)
                elif n >= 2:
                    act.wait_ge(freed_dve, dve_freed_layer[n // 2 - 1])
                src = xn if kind == "mem" else x
                nt = nt or NT
                for t in range(nt):
                    link(act.activation(PJ[t % 2][:], src[:, t, :], ACT.Square, accum_out=ss[:, t:t + 1]))
                act.wait_ge(s_eps, 1)
                if n > 0:
                    act.wait_ge(n_ms, n)
                act.activation(sd[:, 0:nt], ss[:, 0:nt], ACT.Sqrt, scale=1.0 / D, bias=epst).then_inc(n_sd, 1)

            def norm_hi(n):
                kind, nt = NORMS[n]
                dst = mT_hi if kind == "mem" else hT_hi
                for q in range(2 * nt):
                    t, hf = q // 2, q % 2
                    act.wait_ge(n_tr, 2 * tiles_before[n] + q + 1)
                    act.activation(dst[:, 4 * hf:4 * hf + 4, t * P:(t + 1) * P],
                                   PB[q % 4][:].rearrange("p (a b) -> p a b", a=4), ACT.Copy).then_inc(n_hi, 1)

            def narrow_out(n, w):
                act.wait_ge(nr_mm, n + 1)
                act.activation(nT[0:w, :], PB[1][0:w, :], ACT.Copy).then_inc(nr_sb, 1)

            def forget_logs():
                act.wait_ge(f_in, 1)
                link(act.activation(absf, logf, ACT.Abs))
                link(act.activation(absf, absf, ACT.Exp, scale=-1.0))
                act.activation(absf, absf, ACT.Ln, bias=1.0).then_inc(f_ln, 1)

            def forget_out():
                act.wait_ge(f_cum, 1)
                act.activation(negc[:], PB[1][0:NMAIN, :], ACT.Copy, scale=-1.0).then_inc(f_neg, 1)

            def slot(k, layer):
                if in_layer(k, layer) and units[k]["kind"] != "ret":
                    un = units[k]
                    act.wait_ge(m_ready, un["soft"] + 1)
                    act.activation(sc[:, k % 2, 0:un["w"]], sc[:, k % 2, 0:un["w"]], ACT.Exp,
                                   bias=mx[:, k % 2:k % 2 + 1], accum_out=rsum[:, k % 2:k % 2 + 1]).then_inc(e_done, 1)
                if in_layer(k - 1, layer) and units[k - 1]["kind"] != "ret":
                    un = units[k - 1]
                    act.wait_ge(t_done, un["soft"] + 1)
                    if k - 1 >= 2:
                        act.wait_ge(v_done, k - 2)
                    act.activation(pT[:, (k - 1) % 2, 0:un["w"]], PT[:, 0:un["w"]], ACT.Copy).then_inc(t_copied, 1)
                if in_layer(k - 2, layer) and units[k - 2]["kind"] == "ret" and units[k - 2]["i"] == NT - 1:
                    un = units[k - 2]
                    act.wait_ge(o_dve, un["head"] + 1)
                    if un["ret"] >= 1:
                        act.wait_ge(og_used, un["ret"])
                    else:
                        act.wait_ge(t_copied, nsoft_of(1))
                        act.wait_ge(v_done, 64 + 16)
                    act.activation(sq[:], PO[:], ACT.Square).then_inc(o_act, 1)
                if in_layer(k - 3, layer) and units[k - 3]["kind"] == "ret" and units[k - 3]["i"] == NT - 1:
                    act.wait_ge(ms_done, units[k - 3]["ret"] + 1)
                    rsqrt(sq[:], PT[:], 1.0 / HD).then_inc(sd_done, 1)

            def evacuate(s):
                st = steps[s]
                L, kind, c, pj = st["layer"], st["kind"], st["c"], PJ[s % 2]
                if kind in ("o", "o2", "ac", "ab"):
                    return
                act.wait_ge(mm_done, s + 1)
                if kind in ("cq", "ck", "cv"):
                    m = conv_steps.index(s)
                    if m >= 2:
                        act.wait_ge(cv_done, m - 1)
                    else:
                        act.wait_ge(s_pad, 1)
                    act.activation(sg[:, m % 2, 3:3 + S], pj[:, 0:S], ACT.Copy).then_inc(freed_act, 1)
                    return
                if kind == "ah":
                    if st["half"]:
                        act.wait_ge(q_fin, 9 + c)
                    act.activation(hb[:, c, :], pj[:, 0:S], ACT.Copy).then_inc(freed_act, 1)
                    return
                if kind == "gz":
                    act.wait_ge(freed_dve, z_freed[tz_before[s] - 1])
                    act.wait_ge(si_done, 12)
                    act.activation(tz2[:], pj[:, 0:S], ACT.Tanh, scale=0.5).then_inc(tz_ready, 1)
                    return
                if kind == "kmT":
                    act.activation(kmT[:, 2 * st["half"] + c, :], pj[:, 0:NM], ACT.Copy).then_inc(freed_act, 1)
                    return
                if kind == "vm":
                    act.activation(vm[:, c, 256 * st["half"]:256 * st["half"] + 256], pj[:, 0:256],
                                   ACT.Copy).then_inc(freed_act, 1)
                    return
                if kind == "z":
                    if tz_before[s]:
                        act.wait_ge(freed_dve, z_freed[tz_before[s] - 1])
                    act.activation(tz[:], pj[:, 0:S], ACT.Tanh, scale=0.5).then_inc(tz_ready, 1)
                    return
                g = st["g"]
                if c == 0 and g >= 2:
                    act.wait_ge(v_done, last_unit(L, g - 2) + 1)
                if kind == "q":
                    act.activation(qT[:, g % 2, c, :], pj[:, 0:S], ACT.Copy).then_inc(freed_act, 1)
                elif kind == "k":
                    act.activation(kT[:, g % 2, c, :], pj[:, 0:S], ACT.Copy).then_inc(freed_act, 1)
                elif kind == "v":
                    act.activation(v[:, g % 2, 2 * c:2 * c + 2, :].rearrange("p a b -> p (a b)"), pj[:, 0:S],
                                   ACT.Copy).then_inc(freed_act, 1)
                elif kind == "rqk":
                    act.activation((qT, kT)[c][:, g % 2, 1, :], pj[:, 0:S], ACT.Copy,
                                   scale=1.0 if c == 0 else RET_SCALE).then_inc(rr_ready, 1)

            def silu_and_square(s):
                if s in conv_steps:
                    m = conv_steps.index(s)
                    act.wait_ge(cv_done, m + 1)
                    y = (gq, gk, gv)[m // 4][:, m % 4, :]
                    if m:
                        act.wait_ge(si_done, m)
                    act.activation(tz2[:], y, ACT.Tanh, scale=0.5).then_inc(tz_ready2, 1)
                if s in norm_steps:
                    r = norm_steps.index(s)
                    if r < 8:
                        act.wait_ge(si_done, r + 1)
                        y = (gq, gk)[r // 4][:, r % 4, :]
                    else:
                        act.wait_ge(freed_dve, steps[s]["freed"][1])
                        y = hb[:, r % 2, :]
                    if r >= 2:
                        act.wait_ge(q_fin, r - 1)
                    act.activation(sq2[:, r % 2, :], y, ACT.Square).then_inc(q_ready, 1)

            def roots(s):
                if s in norm_steps:
                    r = norm_steps.index(s)
                    act.wait_ge(q_sum, r + 1)
                    rsqrt(sq2[:, r % 2, :], PJ[s % 2][:, S:2 * S], 0.25 if r < 8 else 1.0 / 64).then_inc(q_sd, 1)

            def decay_logs():
                act.wait_ge(d_in, 1)
                link(act.activation(bexp.rearrange("p (c h) -> p c h", c=4), ba[:, :, 0:4], ACT.Exp, scale=-1.0))
                link(act.activation(aabs.rearrange("p (c h) -> p c h", c=4), ba[:, :, 4:8], ACT.Abs))
                link(act.activation(aexp, aabs, ACT.Exp, scale=-1.0))
                link(act.activation(nea, fb[:, NMAIN:NMAIN + 4], ACT.Exp))
                act.activation(aabs, aexp, ACT.Ln, bias=1.0).then_inc(d_act, 1)

            def decay_out():
                act.wait_ge(d_cum, 1)
                act.wait_ge(d_gn, 1)
                link(act.activation(egn, gn, ACT.Exp))
                act.activation(gT[:], PB[1][0:4, :], ACT.Copy).then_inc(d_gT, 1)

            def decay_exps():
                act.wait_ge(d_e2, 1)
                link(act.activation(edk, edk, ACT.Exp))
                act.activation(egl, gl, ACT.Exp).then_inc(d_e, 1)

            def decay_exp(n):
                c = n % 4
                act.wait_ge(g_D, n + 1)
                for h in range(4):
                    last = act.activation(dT[:, h * P:(h + 1) * P], dt_[:, h * P:(h + 1) * P], ACT.Exp,
                                          bias=ngn[:, 4 * c + h:4 * c + h + 1])
                last.then_inc(g_dT, 1)

            def delta_net():
                act.wait_ge(q_fin, 12)
                for c in range(4):
                    act.wait_ge(g_tr, c + 1)
                    act.activation(vn[:, c, :], PB[c][:], ACT.Copy, scale=0.5).then_inc(g_vn, 1)
                for c in range(4):
                    decay_exp(c)
                n = 0
                for l in range(NLVL):
                    for c in range(4):
                        act.wait_ge(g_umm, n + 1)
                        if n >= 4:
                            act.wait_ge(g_tmm, n - 3)
                        act.activation(U[:, c, :], PB[c][:], ACT.Copy).then_inc(g_uc, 1)
                        n += 1
                for c in range(4):
                    act.wait_ge(g_nmm, c + 1)
                    act.activation(nw[:, c, :], PB[c][:], ACT.Copy).then_inc(g_nw, 1)
                for c in range(4):
                    decay_exp(4 + c)
                act.wait_ge(g_iT, 4)
                act.activation(gbr, gbr, ACT.Exp).then_inc(g_eg, 1)
                for c in range(4):
                    act.wait_ge(g_omm, c + 1)
                    act.activation(ob[:, :, c * P:(c + 1) * P], PB[1][:].rearrange("p (h n) -> p h n", h=4),
                                   ACT.Copy).then_inc(g_oe, 1)
                act.wait_ge(g_oe, 4)
                for h in range(4):
                    act.activation(kg[:, h, :], ob[:, h, :], ACT.Square).then_inc(y_sq, 1)
                for h in range(4):
                    act.wait_ge(y_ms, h + 1)
                    rsqrt(kg[:, h, :], PB[h][:], 1.0 / HD).then_inc(y_sd, 1)

            for s, st in enumerate(steps):
                L = st["layer"]
                if s == 0 or steps[s - 1]["layer"] != L:
                    norm_squares(2 * L)
                    if L == 0:
                        for j in range(panels[0]["n"]):
                            split_hi(0, j)
                    norm_hi(2 * L)
                    norm_squares(2 * L + 1)
                    if L == 0:
                        act.wait_ge(s_const, 64)
                        act.activation(wn_hi[:], wn_raw[:], ACT.Copy).then_inc(s_wn, 1)
                        for j in range(panels[1]["n"]):
                            split_hi(1, j)
                    norm_hi(2 * L + 1)
                    if L == 0:
                        narrow_out(0, NMAIN)
                    if L == 2:
                        narrow_out(1, 8)
                if s == gdn_step:
                    delta_net()
                for k in st["slots"][:1]:
                    slot(k, L)
                evacuate(s)
                if st["panel"] + 2 < NPANEL:
                    nn = panels[st["panel"] + 2]["n"]
                    for j in range(nn):
                        if j * st["n"] // nn == st["c"]:
                            split_hi(st["panel"] + 2, j)
                for k in st["slots"][1:]:
                    slot(k, L)
                stages = {(0, 2): forget_logs, (0, 5): forget_out,
                          (2, 2): decay_logs, (2, 5): decay_out, (2, 10): decay_exps}
                if (L, s - layer_first[L]) in stages:
                    stages[L, s - layer_first[L]]()
                if L == 2:
                    silu_and_square(s)
                    roots(s - 1)

            norm_squares(6)
            norm_hi(6)
            narrow_out(2, 36)
            act.wait_ge(r_g, 1)
            act.activation(fld["ge"], fld["gs"], ACT.Exp).then_inc(r_e, 1)
            act.wait_ge(r_d, 1)
            act.activation(de, de, ACT.Exp).then_inc(r_e, 1)

            def mhi(slot, sp_slot, full, value, used, done):
                act.wait_ge(full[slot], value)
                if used is not None:
                    act.wait_ge(used[0], used[1])
                act.activation(w_hi[:, sp_slot, :], m_raw[:, slot, :], ACT.Copy).then_inc(done, 1)

            def mhi_main(e, j):
                if isinstance(e, int):
                    n = 4 + 6 * (e - 1) + j if e else j
                    mhi(n % MRAW, n % SPLIT, m_full, 16 * (n // MRAW + 1), (m_mm, n - 2) if n >= 3 else None, m_hi)
                else:
                    mhi((4 + j) % MRAW, (4 + j) % SPLIT, m_full, e * 16 + 16 * ((4 + j) // MRAW),
                        (m_mm, e * 6 + (j - 4)), m_hi)

            def block_hi(e):
                act.wait_ge(x_tr, e + 1)
                act.activation(xT_hi[:].rearrange("p a b -> p (a b)"), PB[0][:], ACT.Copy).then_inc(x_hi, 1)

            def hidden_tanh(e, mm, value):
                act.wait_ge(mm, value)
                act.activation(mtz[0:CAP, :], PJ[0][0:CAP, 0:FF], ACT.Tanh, scale=0.5).then_inc(h_th, 1)

            def hidden_hi(e):
                act.wait_ge(h_tr, e + 1)
                act.activation(mT_h[:].rearrange("p a b -> p (a b)"), PB[2][:, 0:4 * CAP], ACT.Copy).then_inc(h_hi, 1)

            def store_block(e, mm, value, first=False):
                act.wait_ge(mm, value)
                if not first:
                    act.wait_ge(y_st, e * 16)
                act.activation(ys[0:CAP, :], PJ[1][0:CAP, :], ACT.Copy).then_inc(y_ev, 1)
                act.wait_ge(y_ev, e + 1)
                rows = slice(e * CAP, e * CAP + CAP) if isinstance(e, int) else bass.ds(e * CAP, CAP)
                act.dma_start(A["scr_y"][rows, :], ys[0:CAP, :]).then_inc(y_st, 16)

            def iteration(e, first=False):
                nb = e * 6 + (4 - 6)
                hidden_hi(e - 1)
                for j in (2, 3, 4, 5):
                    mhi_main(e, j)
                hidden_tanh(e, m_mm, nb + 2)
                block_hi(e + 1)
                for j in (0, 1):
                    mhi_main(e + 1, j)
                store_block(e - 1, m_mm, nb + 6, first)

            mhi_main(0, 0)
            mhi_main(0, 1)
            act.wait_ge(r_ix, 16)
            block_hi(0)
            mhi_main(0, 2)
            mhi_main(0, 3)
            hidden_tanh(0, m_mm, 2)
            block_hi(1)
            mhi_main(1, 0)
            mhi_main(1, 1)
            iteration(1, True)
            with act.Fori(2, NE) as e:
                iteration(e)
            hidden_hi(NE - 1)
            store_block(NE - 1, m_mm, 6 * NE)
            with act.register("act_nov") as r:
                act.reg_load(r, ov[0:1, NOV:NOV + 1])
                with act.If(act.snap(r) > 0):
                    with act.Fori(0, NOV) as b:
                        for j in range(6):
                            mhi(j, j % SPLIT, o_full, b * 16 + 16, (o_mm, b * 6 + (j - 2)) if j >= 3 else None, o_hi)
                        hidden_tanh(b + NE, o_mm, b * 6 + 2)
                        block_hi(b + (NE + 1))
                        hidden_hi(b + NE)
                        store_block(b + NE, o_mm, b * 6 + 6)
            for t in range(NT):
                act.wait_ge(c_x, 2 * t + 2)
                link(act.activation(PJ[t % 2][:], x[:, t, :], ACT.Square, accum_out=ss[:, t:t + 1]))
                act.activation(sd[:, t:t + 1], ss[:, t:t + 1], ACT.Sqrt, scale=1.0 / D,
                               bias=epst).then_inc(n_sd, 1)

        @block.vector
        def _(dve):
            ch = [0]

            def link(ins):
                ch[0] += 1
                ins.then_inc(v_ch, 1)
                dve.wait_ge(v_ch, ch[0])

            def split_lo(n, j):
                cnt = panels[n]["n"]
                w = PANEL // cnt
                dve.wait_ge(hi_done, (pieces[n - 1] if n else 0) + j + 1)
                dve.tensor_tensor(w_lo[:, n % SPLIT, j * w:(j + 1) * w], w_raw[:, n % RAW, j * w:(j + 1) * w],
                                  w_hi[:, n % SPLIT, j * w:(j + 1) * w].bitcast(F32),
                                  ALU.subtract).then_inc(lo_done, 1)

            def norm_scale(n):
                kind, nt = NORMS[n]
                src = xn if kind == "mem" else x
                dve.wait_ge(n_sd, n + 1)
                ins = dve.reciprocal(rstd[:, 0:nt or NT], sd[:, 0:nt or NT])
                ins.then_inc(n_ms, 1)
                dve.wait_ge(n_ms, n + 1)
                gain_wait(dve, gains_before[n])
                if kind == "self":
                    for t in range(NT):
                        dve.scalar_tensor_tensor(x[:, t, :], x[:, t, :], rstd[:, t:t + 1], gbc[:],
                                                 ALU.mult, ALU.mult).then_inc(s_x1, 1)
                    return
                if n == 5:
                    dve.wait_ge(s_x1, 4)
                for t in range(nt):
                    if n == 6 and t >= 2:
                        dve.wait_ge(hn_st[t % 2], 16 * (t // 2))
                    if kind == "x" and t >= 2:
                        dve.wait_ge(n_tr, 2 * (tiles_before[n] + t - 1))
                    elif kind == "x" and n < 5:
                        dve.wait_ge(n_tr, 2 * (tiles_before[n - 1] + t + 1))
                    dve.scalar_tensor_tensor(xn[:, t % 2, :], src[:, t, :], rstd[:, t:t + 1], gbc[:],
                                             ALU.mult, ALU.mult).then_inc(n_xn, 1)
                    if t >= 1:
                        norm_lo(n, t - 1)
                norm_lo(n, nt - 1)

            def norm_lo(n, t):
                kind, nt = NORMS[n]
                hi, lo = (mT_hi, mT_lo) if kind == "mem" else (hT_hi, hT_lo)
                for hf in range(2):
                    q = 2 * t + hf
                    dve.wait_ge(n_hi, 2 * tiles_before[n] + q + 1)
                    dve.tensor_tensor(lo[:, 4 * hf:4 * hf + 4, t * P:(t + 1) * P],
                                      PB[q % 4][:].rearrange("p (a b) -> p a b", a=4),
                                      hi[:, 4 * hf:4 * hf + 4, t * P:(t + 1) * P].bitcast(F32),
                                      ALU.subtract).then_inc(n_lo, 1)

            def forget_in():
                dve.wait_ge(f_mm, 1)
                dve.tensor_tensor(logf.rearrange("p (t h) -> p t h", t=NT),
                                  PB[0][:, 0:48].rearrange("p (t h) -> p t h", t=NT),
                                  fb[:, 0:NMAIN].unsqueeze(1).broadcast_to([P, NT, NMAIN]),
                                  ALU.add).then_inc(f_in, 1)

            def forget_log():
                dve.wait_ge(f_ln, 1)
                dve.scalar_tensor_tensor(logf, logf, 0.0, absf, ALU.min, ALU.subtract).then_inc(f_log, 1)

            def soft1(k):
                un = units[k]
                w, b = un["w"], k % 2
                dve.wait_ge(s_ready, k + 1)
                if un["soft"] >= 2:
                    dve.wait_ge(t_done, un["soft"] - 1)
                if un["kind"] == "fox":
                    dve.wait_ge(aux_full[un["g"] % 2], 16 * (un["g"] // 2))
                    ins = dve.scalar_tensor_tensor(sc[:, b, 0:w], PS[b][:, 0:w], QK_SCALE,
                                                   aux[:, un["g"] % 2, un["h"], 0:w], ALU.mult, ALU.add)
                else:
                    ins = dve.tensor_scalar(sc[:, b, 0:w], PS[b][:, 0:w], QK_SCALE, None, ALU.mult)
                ins.then_inc(s_read, 1)
                dve.wait_ge(s_read, k + 1)
                if un["kind"] == "fox":
                    link(dve.tensor_tensor(sc[:, b, w - P:w], sc[:, b, w - P:w], cst[:, C_CM:C_CM + P], ALU.add))
                dve.tensor_reduce(mx[:, b:b + 1], sc[:, b, 0:w], AX.X, ALU.max, negate=True).then_inc(m_ready, 1)

            def soft2(k):
                un = units[k]
                w, b = un["w"], k % 2
                dve.wait_ge(e_done, un["soft"] + 1)
                link(dve.reciprocal(rinv[:, b:b + 1], rsum[:, b:b + 1]))
                dve.tensor_scalar(sc[:, b, 0:w], sc[:, b, 0:w], rinv[:, b:b + 1], None, ALU.mult).then_inc(p_ready, 1)

            def decay(k):
                un = units[k]
                w, b, g = un["w"], k % 2, un["g"]
                dve.wait_ge(s_ready, k + 1)
                dve.wait_ge(aux_full[g % 2], 48 + 16 * (g // 2))
                dve.wait_ge(v_done, k - 1)
                dve.tensor_tensor(sc[:, b, 0:w], PS[b][:, 0:w], aux[:, g % 2, un["h"], 0:w],
                                  ALU.mult).then_inc(s_read, 1)

            def gate(k):
                un = units[k]
                L, g, h = un["layer"], un["g"], un["h"]
                par = g % 2
                dve.wait_ge(v_done, k + 1)
                last = dve.scalar_tensor_tensor(og[:], PO[:], 0.5, zs[:, par, h, :], ALU.mult, ALU.mult)
                last.then_inc(o_dve, 1)
                dve.wait_ge(o_dve, un["head"] + 1)
                if un["kind"] != "ret":
                    split_head(un)

            def split_head(un):
                L, g, h = un["layer"], un["g"], un["h"]
                par = g % 2
                if h == 0 and g >= 2:
                    dve.wait_ge(mm_done, panel_end(o_panel[(L, g - 2)]))
                link(dve.tensor_copy(oT_hi[:, par, h, :], og[:]))
                dve.tensor_tensor(oT_lo[:, par, h, :], og[:], oT_hi[:, par, h, :].bitcast(F32),
                                  ALU.subtract).then_inc(ot_done, 1)

            def ret_scale(k):
                un = units[k]
                dve.wait_ge(sd_done, un["ret"] + 1)
                dve.tensor_tensor(og[:], og[:], sq[:], ALU.mult).then_inc(og_used, 1)
                dve.wait_ge(og_used, un["ret"] + 1)
                split_head(un)

            def slot_first(k, layer):
                if in_layer(k, layer):
                    if units[k]["kind"] == "ret":
                        decay(k)
                    else:
                        soft1(k)
                if in_layer(k - 2, layer) and units[k - 2]["i"] == NT - 1:
                    gate(k - 2)

            def slot_second(k, layer):
                if in_layer(k, layer) and units[k]["kind"] != "ret":
                    soft2(k)
                if in_layer(k - 3, layer) and units[k - 3]["kind"] == "ret" and units[k - 3]["i"] == NT - 1:
                    ret_scale(k - 3)

            def rotate(s):
                st = steps[s]
                r = rope_no(s)
                dve.wait_ge(perm_done, r + 1)
                if r == 0:
                    gain_wait(dve, 5)
                link(dve.tensor_tensor(rt[:], PJ[s % 2][:, S:2 * S], rope[:, 1, :], ALU.mult))
                buf = (qT, kT)[st["c"]][:, st["g"] % 2]
                link(dve.tensor_tensor(buf[:, 1, :], buf[:, 1, :], rope[:, 0, :], ALU.mult))
                dve.tensor_tensor(buf[:, 0, :], rt[:], buf[:, 1, :], ALU.add).then_inc(freed_dve, 1)

            def evacuate(s):
                st = steps[s]
                kind, c, pj = st["kind"], st["c"], PJ[s % 2]
                if kind == "z":
                    dve.wait_ge(tz_ready, tz_before[s] + 1)
                    dve.scalar_tensor_tensor(zs[:, st["g"] % 2, c, :], tz[:], 1.0, pj[:, 0:S],
                                             ALU.add, ALU.mult).then_inc(freed_dve, 1)
                elif kind == "gz":
                    dve.wait_ge(tz_ready, tz_before[s] + 1)
                    dve.scalar_tensor_tensor(gz[:, 2 * st["half"] + c, :], tz2[:], 1.0, pj[:, 0:S],
                                             ALU.add, ALU.mult).then_inc(freed_dve, 1)
                elif kind in ("cq", "ck", "cv"):
                    m = conv_steps.index(s)
                    dve.wait_ge(freed_act, st["freed"][1])
                    conv((gq, gk, gv)[m // 4][:, m % 4, :], sg[:, m % 2, :], V_DNCONV + 4 * m, 4, cv_done)
                elif kind == "ac":
                    m = a_steps.index(s)
                    dve.wait_ge(mm_done, s + 1)
                    dve.wait_ge(freed_act, steps[s - 2]["freed"][1])
                    dve.tensor_tensor(sg[:, c, 3:3 + S], pj[:, 0:S], hb[:, c, :], ALU.mult).then_inc(freed_dve, 1)
                    dve.wait_ge(freed_dve, st["freed"][1])
                    conv(hb[:, c, :], sg[:, c, 1:], V_ACONV + 3 * m, 3, a_h)
                elif kind == "ab":
                    dve.wait_ge(mm_done, s + 1)
                    dve.wait_ge(a_h, norm_steps.index(s) - 7)
                    dve.tensor_tensor(hb[:, c, :], pj[:, 0:S], hb[:, c, :], ALU.mult).then_inc(freed_dve, 1)
                elif kind in ("o", "o2"):
                    dve.wait_ge(mm_done, s + 1)
                    if st["freed"][1] > 1:
                        dve.wait_ge(freed_dve, st["freed"][1] - 1)
                    dve.tensor_tensor(x[:, c, :], x[:, c, :], pj[:], ALU.add).then_inc(freed_dve, 1)

            def conv(dst, src, w0, width, done):
                link(dve.tensor_scalar(dst, src[:, 0:S], vecs[:, w0:w0 + 1], None, ALU.mult))
                for j in range(1, width):
                    ins = dve.scalar_tensor_tensor(dst, src[:, j:j + S], vecs[:, w0 + j:w0 + j + 1], dst,
                                                   ALU.mult, ALU.add)
                    if j < width - 1:
                        link(ins)
                ins.then_inc(done, 1)

            def silu(s):
                if s in conv_steps:
                    m = conv_steps.index(s)
                    dve.wait_ge(tz_ready2, m + 1)
                    y = (gq, gk, gv)[m // 4][:, m % 4, :]
                    dve.scalar_tensor_tensor(y, tz2[:], 1.0, y, ALU.add, ALU.mult).then_inc(si_done, 1)

            def finish_norm(s):
                if s not in norm_steps:
                    return
                r = norm_steps.index(s)
                q = sq2[:, r % 2, :]
                dve.wait_ge(q_sd, r + 1)
                if r < 8:
                    y = (gq, gk)[r // 4][:, r % 4, :]
                    dve.scalar_tensor_tensor(y, y, 0.5 * QK_SCALE if r < 4 else 0.5, q,
                                             ALU.mult, ALU.mult).then_inc(q_fin, 1)
                else:
                    t = r - 8
                    y = hb[:, r % 2, :]
                    link(dve.scalar_tensor_tensor(y, y, vecs[:, V_ANORM + t:V_ANORM + t + 1], q, ALU.mult, ALU.mult))
                    link(dve.tensor_copy(ya_hi[:, t, :], y))
                    dve.tensor_tensor(ya_lo[:, t, :], y, ya_hi[:, t, :].bitcast(F32), ALU.subtract).then_inc(q_fin, 1)

            def c4(a):
                return a.rearrange("p (c h) -> p c h", c=4)

            def decay_in():
                dve.wait_ge(d_mm, 1)
                raw = PB[0][:, 0:32].rearrange("p (c n) -> p c n", c=4)
                link(dve.tensor_copy(ba[:, :, 0:4], raw[:, :, 0:4]))
                dve.tensor_tensor(ba[:, :, 4:8], raw[:, :, 4:8],
                                  fb[:, NMAIN + 4:NMAIN + 8].unsqueeze(1).broadcast_to([P, 4, 4]),
                                  ALU.add).then_inc(d_in, 1)

            def decay_logs():
                dve.wait_ge(d_act, 1)
                link(dve.tensor_scalar(bexp, bexp, 1.0, None, ALU.add))
                link(dve.reciprocal(beta, bexp))
                link(dve.scalar_tensor_tensor(c4(lg), ba[:, :, 4:8], 0.0, c4(aabs), ALU.max, ALU.add))
                link(dve.tensor_tensor(c4(lg), c4(lg), nea.unsqueeze(1).broadcast_to([P, 4, 4]), ALU.mult))
                dve.tensor_scalar(lg, lg, -1.0, None, ALU.mult).then_inc(d_gate, 1)

            def decay_out():
                dve.wait_ge(d_cum, 1)
                link(dve.tensor_copy(gn, PB[0][:, 0:16]))
                dve.tensor_scalar(ngn, gn, -1.0, None, ALU.mult).then_inc(d_gn, 1)

            def decay_ends():
                dve.wait_ge(d_gb, 16)
                for c in range(4):
                    ins = dve.tensor_copy(gl[:, 4 * c:4 * c + 4], gbr[:, :, c * P + P - 1])
                link(ins)
                dve.tensor_tensor(edk, gl, gn, ALU.subtract).then_inc(d_e2, 1)

            def heads(t):
                return t.rearrange("p (h n) -> p h n", h=4)

            def per_head(col, c):
                return col[:, 4 * c:4 * c + 4].unsqueeze(2).broadcast_to([P, 4, P])

            def decay_mask(n):
                c = n % 4
                if n >= 1:
                    dve.wait_ge(g_dT, n)
                dve.tensor_tensor(heads(dt_[:]), gbr[:, :, c * P:(c + 1) * P],
                                  cst[:, C_CMT:C_CMT + P].unsqueeze(1).broadcast_to([P, 4, P]),
                                  ALU.add).then_inc(g_D, 1)

            def delta_net():
                dve.wait_ge(d_e, 1)
                link(dve.tensor_scalar(bexp, egn, -1.0, None, ALU.mult))
                for c in range(4):
                    b = PB[c]
                    dve.wait_ge(g_tr, 5 + c)
                    link(dve.tensor_tensor(heads(kg[:, c, :]), heads(b[:]), per_head(bexp, c), ALU.mult))
                    dve.tensor_tensor(heads(kd[:, c, :]), heads(b[:]), per_head(edk, c), ALU.mult).then_inc(g_kg, 1)
                for c in range(4):
                    decay_mask(c)
                    dve.wait_ge(g_dT, c + 1)
                    dve.wait_ge(g_kk, c + 1)
                    link(dve.tensor_tensor(LT[:, c, :], PB[c][:], dT[:], ALU.mult))
                    dve.tensor_tensor(heads(LT[:, c, :]), heads(LT[:, c, :]), per_head(beta, c),
                                      ALU.mult).then_inc(g_LT, 1)
                ones = ident.unsqueeze(1).broadcast_to([P, 4, P])
                for c in range(4):
                    dve.tensor_copy(heads(T_[:, c, :]), ones)
                    dve.tensor_copy(heads(TT[:, c, :]), ones).then_inc(g_tup, 1)
                n = 0
                for l in range(NLVL):
                    for c in range(4):
                        dve.wait_ge(g_tup, n + 1)
                        dve.wait_ge(g_tmm, n + 1)
                        if l < NLVL - 1:
                            dve.tensor_tensor(T_[:, c, :], T_[:, c, :], PJ[c // 2][:, (c % 2) * S:(c % 2 + 1) * S],
                                              ALU.subtract)
                        dve.tensor_tensor(TT[:, c, :], TT[:, c, :], PB[c][:], ALU.subtract).then_inc(g_tup, 1)
                        n += 1
                for c in range(4):
                    decay_mask(4 + c)
                    dve.wait_ge(g_dT, 5 + c)
                    dve.wait_ge(g_imm, c + 1)
                    dve.tensor_tensor(iT[:, c, :], PJ[c // 2][:, (c % 2) * S:(c % 2 + 1) * S], dT[:],
                                      ALU.mult).then_inc(g_iT, 1)
                dve.wait_ge(g_eg, 1)
                dve.tensor_tensor(gq[:].rearrange("p h n -> p (h n)"), gq[:].rearrange("p h n -> p (h n)"),
                                  gbr.rearrange("p h n -> p (h n)"), ALU.mult).then_inc(g_qd, 1)
                for c in range(4):
                    dve.wait_ge(g_vmm, c + 1)
                    dve.tensor_tensor(heads(vnw[:, c % 2, :]), heads(PB[0][:]), per_head(beta, c),
                                      ALU.mult).then_inc(g_vne, 1)
                    if c < 3:
                        dve.wait_ge(g_smm, c + 1)
                        if c == 0:
                            dve.tensor_copy(SS[:, 1, :], PB[2][:]).then_inc(g_se, 1)
                        else:
                            dve.wait_ge(g_se, c)
                            new = SS[:, (c + 1) % 2, :]
                            link(dve.tensor_tensor(heads(new), heads(SS[:, c % 2, :]), per_head(egl, c), ALU.mult))
                            dve.tensor_tensor(new, new, PB[2][:], ALU.add).then_inc(g_se, 1)
                for h in range(4):
                    dve.wait_ge(y_sd, h + 1)
                    link(dve.scalar_tensor_tensor(gz[:, h, :], gz[:, h, :], vecs[:, V_DNNORM:V_DNNORM + 1],
                                                  kg[:, h, :], ALU.mult, ALU.mult))
                    link(dve.scalar_tensor_tensor(gz[:, h, :], gz[:, h, :], 0.5, ob[:, h, :], ALU.mult, ALU.mult))
                    link(dve.tensor_copy(yb_hi[:, h, :], gz[:, h, :]))
                    dve.tensor_tensor(yb_lo[:, h, :], gz[:, h, :], yb_hi[:, h, :].bitcast(F32),
                                      ALU.subtract).then_inc(y_fin, 1)

            dve.memset(epst, EPS).then_inc(s_eps, 1)
            for s, st in enumerate(steps):
                L = st["layer"]
                if s == 0 or steps[s - 1]["layer"] != L:
                    norm_scale(2 * L)
                    if L == 0:
                        for j in range(panels[0]["n"]):
                            split_lo(0, j)
                    norm_scale(2 * L + 1)
                    if L == 0:
                        dve.wait_ge(s_wn, 1)
                        dve.tensor_tensor(wn_lo[:], wn_raw[:], wn_hi[:].bitcast(F32), ALU.subtract).then_inc(s_wn, 1)
                        for j in range(panels[1]["n"]):
                            split_lo(1, j)
                    if L == 2:
                        dve.memset(sg[:, :, 0:3], 0.0).then_inc(s_pad, 1)
                if s == gdn_step:
                    delta_net()
                if s >= 1 and steps[s - 1]["kind"] == "rqk":
                    rotate(s - 1)
                nn = panels[st["panel"] + 2]["n"] if st["panel"] + 2 < NPANEL else 0
                lo = [j for j in range(nn) if j * st["n"] // nn == st["c"]]
                if not st["slots"]:
                    evacuate(s)
                for k in st["slots"]:
                    slot_first(k, L)
                    if k == st["slots"][0]:
                        evacuate(s)
                        for j in lo:
                            split_lo(st["panel"] + 2, j)
                        lo = []
                    slot_second(k, L)
                for j in lo:
                    split_lo(st["panel"] + 2, j)
                stages = {(0, 1): forget_in, (0, 3): forget_log,
                          (2, 1): decay_in, (2, 3): decay_logs, (2, 5): decay_out, (2, 10): decay_ends}
                if (L, s - layer_first[L]) in stages:
                    stages[L, s - layer_first[L]]()
                if L == 2:
                    silu(s)
                    finish_norm(s - 1)

            norm_scale(6)
            F = fld

            def tt(o, a, b, op):
                link(dve.tensor_tensor(o, a, b, op))

            def red(o, a, op):
                link(dve.tensor_reduce(o, a, AX.X, op))

            def wide(a, n):
                return a.unsqueeze(2).broadcast_to([P, NT, n])

            def first_max(values, n, mx_, w, oh, weights):
                red(mx_, values, ALU.max)
                tt(w, values, wide(mx_, n), ALU.is_equal)
                tt(w, w, weights.unsqueeze(1).broadcast_to([P, NT, n]), ALU.mult)
                red(gpm, w, ALU.max)
                tt(oh, w, wide(gpm, n), ALU.is_equal)

            dve.wait_ge(r_mm, 1)
            link(dve.tensor_copy(F["L"], PB[0][:, 0:36 * NT].rearrange("p (t n) -> p t n", t=NT)))
            Lg = F["L"][:, :, 0:NG]
            first_max(Lg, NG, gmx, F["gw"], F["goh"], rowc[:, R_W4:R_W4 + NG])
            dve.tensor_tensor(F["gs"], Lg, wide(gmx, NG), ALU.subtract).then_inc(r_g, 1)
            ge = F["t4"].rearrange("p t (g e) -> p t g e", g=NG)
            for g in range(NG):
                tt(ge[:, :, g, :], F["L"][:, :, NG + EPG * g:NG + EPG * (g + 1)],
                   F["goh"][:, :, g:g + 1].broadcast_to([P, NT, EPG]), ALU.mult)
            red(F["sel"], F["t4"].rearrange("p t (g e) -> p t e g", g=NG), ALU.add)
            w8 = rowc[:, R_W8:R_W8 + EPG]
            first_max(F["sel"], EPG, m0, F["w8"], F["oh0"], w8)
            link(dve.scalar_tensor_tensor(F["sel"], F["oh0"], NEG, F["sel"], ALU.mult, ALU.add))
            first_max(F["sel"], EPG, m1, F["w8"], F["oh1"], w8)
            dve.wait_ge(r_e, 1)
            dve.tensor_tensor(de, m1, m0, ALU.subtract).then_inc(r_d, 1)
            for i in range(2):
                Ei = F[f"E{i}"]
                for g in range(NG):
                    tt(Ei[:, :, EPG * g:EPG * (g + 1)], F[f"oh{i}"],
                       F["goh"][:, :, g:g + 1].broadcast_to([P, NT, EPG]), ALU.mult)
            dve.tensor_tensor(F["E"], F["E0"], F["E1"], ALU.add).then_inc(r_E, 1)
            red(gsum, F["ge"], ALU.add)
            link(dve.reciprocal(gp, gsum))
            dve.wait_ge(r_e, 2)
            link(dve.tensor_scalar(gsum, de, 1.0, None, ALU.add))
            link(dve.reciprocal(gsum, gsum))
            tt(gates[:, 0:4], gp, gsum, ALU.mult)
            tt(gates[:, 4:8], gates[:, 0:4], de, ALU.mult)
            dve.wait_ge(r_rk, 1)
            link(dve.tensor_copy(cnt, PB[1][:, NT * NE:(NT + 1) * NE]))
            link(dve.tensor_scalar(ovc, cnt, float(CAP), None, ALU.is_gt))
            for m in range(2, -(-S // CAP)):
                link(dve.scalar_tensor_tensor(ovc, cnt, float(m * CAP), ovc, ALU.is_gt, ALU.add))
            link(dve.tensor_tensor_scan(ovi, cst[:, C_ONE:C_ONE + NE], ovc, 0.0, ALU.mult, ALU.add))
            tt(ove, ovi, ovc, ALU.subtract)
            c7 = cmp7.rearrange("p (j e) -> p j e", j=NOV)
            tt(c7, ovi.unsqueeze(1).broadcast_to([P, NOV, NE]),
               rowc[:, R_J:R_J + NOV].unsqueeze(2).broadcast_to([P, NOV, NE]), ALU.is_le)
            link(dve.tensor_reduce(cx[:, 0:NOV], c7, AX.X, ALU.add))
            link(dve.tensor_scalar(cx[:, 0:NOV], cx[:, 0:NOV], float(NE - 1), None, ALU.min))
            link(dve.tensor_copy(cx[:, NOV:NOV + 1], ovi[:, NE - 1:NE]))
            dve.tensor_copy(ov[:], cx).then_inc(r_ov, 1)
            for i in range(2):
                Ei, sl = F[f"E{i}"], slice(4 * i, 4 * i + 4)
                tt(F["tm"], Ei, PB[1][:, 0:NT * NE].rearrange("p (t n) -> p t n", t=NT), ALU.mult)
                red(rk[:, sl], F["tm"], ALU.add)
                tt(F["tm"], Ei, ove.unsqueeze(1).broadcast_to([P, NT, NE]), ALU.mult)
                red(ovk[:, sl], F["tm"], ALU.add)
                tt(F["tm"], Ei, rowc[:, R_I32:R_I32 + NE].unsqueeze(1).broadcast_to([P, NT, NE]), ALU.mult)
                red(ek[:, sl], F["tm"], ALU.add)
            link(dve.tensor_scalar(qk_, rk, float(CAP), None, ALU.is_ge))
            for m in range(2, -(-S // CAP)):
                link(dve.scalar_tensor_tensor(qk_, rk, float(m * CAP), qk_, ALU.is_ge, ALU.add))
            link(dve.scalar_tensor_tensor(rk, qk_, -float(CAP), rk, ALU.mult, ALU.add))
            tt(blk, ovk, qk_, ALU.add)
            link(dve.scalar_tensor_tensor(blk, blk, float(NE - 1), ek, ALU.add, ALU.subtract))
            link(dve.tensor_scalar(tq, qk_, 1.0, None, ALU.min))
            tt(blk, blk, tq, ALU.mult)
            tt(blk, blk, ek, ALU.add)
            link(dve.scalar_tensor_tensor(tq, rk, float(NB), blk, ALU.mult, ALU.add))
            link(dve.tensor_copy(di[:], tq))
            link(dve.scalar_tensor_tensor(tq, blk, float(CAP), rk, ALU.mult, ALU.add))
            dve.tensor_copy(yi[:], tq).then_inc(r_dst, 1)

            def mlo(slot, sp_slot, hi, value, done):
                dve.wait_ge(hi, value)
                dve.tensor_tensor(w_lo[:, sp_slot, :], m_raw[:, slot, :], w_hi[:, sp_slot, :].bitcast(F32),
                                  ALU.subtract).then_inc(done, 1)

            def mlo_main(e, j):
                if isinstance(e, int):
                    n = 4 + 6 * (e - 1) + j if e else j
                    mlo(n % MRAW, n % SPLIT, m_hi, n + 1, m_lo)
                else:
                    mlo((4 + j) % MRAW, (4 + j) % SPLIT, m_hi, e * 6 + (j - 1), m_lo)

            def block_lo(e):
                dve.wait_ge(x_hi, e + 1)
                dve.tensor_tensor(xT_lo[:].rearrange("p a b -> p (a b)"), PB[0][:],
                                  xT_hi[:].rearrange("p a b -> p (a b)").bitcast(F32),
                                  ALU.subtract).then_inc(x_lo, 1)

            def hidden_mid(e, mm, value):
                dve.wait_ge(h_th, e + 1)
                link_free(dve.scalar_tensor_tensor(msl[0:CAP, :], mtz[0:CAP, :], 1.0, PJ[0][0:CAP, 0:FF], ALU.add, ALU.mult), e)
                dve.wait_ge(mm, value)
                dve.scalar_tensor_tensor(mid[0:CAP, :], msl[0:CAP, :], 0.5, PJ[0][0:CAP, FF:2 * FF], ALU.mult,
                                         ALU.mult).then_inc(h_mid, 1)

            def link_free(ins, e):
                ins.then_inc(h_sl, 1)
                dve.wait_ge(h_sl, e + 1)

            def hidden_lo(e):
                dve.wait_ge(h_hi, e + 1)
                dve.tensor_tensor(mT_l[:].rearrange("p a b -> p (a b)"), PB[2][:, 0:4 * CAP],
                                  mT_h[:].rearrange("p a b -> p (a b)").bitcast(F32), ALU.subtract).then_inc(h_lo, 1)

            mlo_main(0, 0)
            mlo_main(0, 1)
            block_lo(0)
            mlo_main(0, 2)
            mlo_main(0, 3)
            hidden_mid(0, m_mm, 4)
            block_lo(1)
            mlo_main(1, 0)
            mlo_main(1, 1)
            with dve.Fori(1, NE) as e:
                hidden_lo(e - 1)
                for j in (2, 3, 4, 5):
                    mlo_main(e, j)
                hidden_mid(e, m_mm, e * 6 + 2)
                block_lo(e + 1)
                for j in (0, 1):
                    mlo_main(e + 1, j)
            hidden_lo(NE - 1)
            with dve.register("dve_nov") as r:
                dve.reg_load(r, ov[0:1, NOV:NOV + 1])
                with dve.If(dve.snap(r) > 0):
                    with dve.Fori(0, NOV) as b:
                        for j in range(6):
                            mlo(j, j % SPLIT, o_hi, b * 6 + (j + 1), o_lo)
                        hidden_mid(b + NE, o_mm, b * 6 + 4)
                        block_lo(b + (NE + 1))
                        hidden_lo(b + NE)
            def combine(t):
                for n in (2 * t, 2 * t + 1):
                    i = n % 2 * NT + t
                    dve.wait_ge(c_g[n], 16)
                    if n % 2:
                        dve.wait_ge(c_x, n)
                    dve.scalar_tensor_tensor(x[:, t, :], yg[:, n, :], gates[:, i:i + 1], x[:, t, :],
                                             ALU.mult, ALU.add).then_inc(c_x, 1)

            def last_norm(t):
                dve.wait_ge(n_sd, 7 + t + 1)
                link(dve.reciprocal(rstd[:, t:t + 1], sd[:, t:t + 1]))
                dve.scalar_tensor_tensor(x[:, t, :], x[:, t, :], rstd[:, t:t + 1], gbc[:],
                                         ALU.mult, ALU.mult).then_inc(s_x1, 1)

            gain_wait(dve, gains_before[7])
            for t in range(NT):
                combine(t)
                if t:
                    last_norm(t - 1)
            last_norm(NT - 1)

        @block.tensor
        def _(pe):
            def norm_transpose(n):
                kind, nt = NORMS[n]
                for q in range(2 * nt):
                    t, hf = q // 2, q % 2
                    if hf == 0:
                        pe.wait_ge(n_xn, tiles_before[n] + t + 1)
                    if q >= 4 or n:
                        pe.wait_ge(n_lo, 2 * tiles_before[n] + max(q - 3, 0))
                    for a in range(4):
                        k = 4 * hf + a
                        last = pe.transpose(PB[q % 4][:, a * P:(a + 1) * P], xn[:, t % 2, k * P:(k + 1) * P], ident)
                    last.then_inc(n_tr, 1)

            def narrow(n, c0, w):
                for k in range(KD):
                    last = mm3(pe, PB[1][0:w, :], (wn_hi[:, k, c0:c0 + w], wn_lo[:, k, c0:c0 + w]),
                               (hT_hi[:, k, :], hT_lo[:, k, :]), k == 0, k == KD - 1)
                last.then_inc(nr_mm, 1)

            def narrow_transpose(n, w):
                pe.wait_ge(nr_sb, n + 1)
                for t in range(NT):
                    last = pe.transpose(PB[0][:, t * w:(t + 1) * w], nT[0:w, t * P:(t + 1) * P], ident[0:w, 0:w])
                return last

            def forget_sums():
                pe.wait_ge(f_log, 1)
                for t in range(NT):
                    for j in range(t + 1):
                        c0 = C_TRI if j == t else C_ONE
                        last = pe.matmul(PB[1][0:NMAIN, t * P:(t + 1) * P], st_[:, j * NMAIN:(j + 1) * NMAIN],
                                         cst[:, c0:c0 + P], start=(j == 0), stop=(j == t))
                last.then_inc(f_cum, 1)

            def products(s, middle):
                st = steps[s]
                kind, c, n = st["kind"], st["c"], st["panel"]
                pj = PJ[s % 2]
                if c == 0:
                    pe.wait_ge(lo_done, pieces[n])
                if s >= 2:
                    who, cnt = steps[s - 2]["freed"]
                    pe.wait_ge(freed[who], cnt)
                if kind in ("kmT", "q", "k", "rqk", "z", "cq", "ck", "cv", "gz", "ah", "ac", "ab"):
                    wh, wl = w_view(n, KD)
                    rh, rl = (mT_hi, mT_lo) if kind == "kmT" else (hT_hi, hT_lo)
                    wd = NM if kind == "kmT" else S
                    for k in range(KD):
                        if k == KD // 2:
                            for u in middle:
                                slot(u, st["layer"])
                        last = mm3(pe, pj[:, 0:wd], (wh[:, k, c * P:(c + 1) * P], wl[:, k, c * P:(c + 1) * P]),
                                   (rh[:, k, :], rl[:, k, :]), k == 0, k == KD - 1)
                elif kind == "vm":
                    wh, wl = w_view(n, KD)
                    for k in range(KD):
                        last = mm3(pe, pj[:, 0:256], (mT_hi[:, k, c * P:(c + 1) * P], mT_lo[:, k, c * P:(c + 1) * P]),
                                   (wh[:, k, :], wl[:, k, :]), k == 0, k == KD - 1)
                elif kind == "v":
                    wh, wl = w_view(n, KD)
                    for a in range(2):
                        t = 2 * c + a
                        for k in range(KD):
                            last = mm3(pe, pj[:, 256 * a:256 * a + 256],
                                       (hT_hi[:, k, t * P:(t + 1) * P], hT_lo[:, k, t * P:(t + 1) * P]),
                                       (wh[:, k, :], wl[:, k, :]), k == 0, k == KD - 1)
                elif kind == "o2":
                    wh, wl = w_view(n, 2)
                    k0 = 2 * (st["g"] % 2)
                    if s - o2_first < 2:
                        pe.wait_ge(q_sd, 11 + s - o2_first)
                    lh, ll = (ya_hi, ya_lo) if st["g"] < 2 else (yb_hi, yb_lo)
                    if c == 0:
                        if st["g"] < 2:
                            pe.wait_ge(q_fin, 10 + 2 * st["g"])
                        else:
                            pe.wait_ge(y_fin, 2 * (st["g"] - 1))
                    for hf in range(2):
                        for k in range(2):
                            last = mm3(pe, pj[:, hf * S:(hf + 1) * S],
                                       (lh[:, k0 + k, c * P:(c + 1) * P], ll[:, k0 + k, c * P:(c + 1) * P]),
                                       (wh[:, k, hf * S:(hf + 1) * S], wl[:, k, hf * S:(hf + 1) * S]),
                                       k == 0, k == 1)
                elif kind == "o":
                    wh, wl = w_view(n, 2)
                    par = st["g"] % 2
                    if c == 0:
                        pe.wait_ge(ot_done, 16 * st["layer"] + 2 * (st["g"] + 1))
                    for hf in range(2):
                        for k in range(2):
                            last = mm3(pe, pj[:, hf * S:(hf + 1) * S],
                                       (oT_hi[:, par, k, c * P:(c + 1) * P], oT_lo[:, par, k, c * P:(c + 1) * P]),
                                       (wh[:, k, hf * S:(hf + 1) * S], wl[:, k, hf * S:(hf + 1) * S]),
                                       k == 0, k == 1)
                last.then_inc(mm_done, 1)

            def scores(k):
                un = units[k]
                par, h, i, w, b = un["g"] % 2, un["h"], un["i"], un["w"], k % 2
                if h == 0 and i == 0:
                    for who in ("act", "dve"):
                        c = max([st["freed"][1] for st in steps if st["freed"][0] == who and st["layer"] == un["layer"]
                                 and st.get("g") == un["g"] and st["kind"] in ("q", "k", "v", "rqk")] + [0])
                        if c:
                            pe.wait_ge(freed[who], c)
                if k >= 2:
                    pe.wait_ge(s_read, k - 1)
                if k == 1:
                    pe.wait_ge(f_neg, 1)
                qs = slice(i * P, (i + 1) * P)
                if un["kind"] == "fox":
                    last = pe.matmul(PS[b][:, 0:w], qT[:, par, h, qs], kT[:, par, h, 0:w], start=True, stop=True)
                elif un["kind"] == "mem":
                    last = pe.matmul(PS[b][:, 0:w], qT[:, par, h, qs], kmT[:, 2 * un["g"] + h, :], start=True, stop=True)
                else:
                    hp = slice(64 * h, 64 * h + 64)
                    last = pe.matmul(PS[b][:, 0:w], kT[hp, par, 0, qs], qT[hp, par, 0, i * P:S], start=True, stop=True)
                last.then_inc(s_ready, 1)

            def transposes(k):
                un = units[k]
                pe.wait_ge(p_ready, un["soft"] + 1)
                if un["soft"] >= 1:
                    pe.wait_ge(t_copied, un["soft"])
                for a in range(un["w"] // P):
                    last = pe.transpose(PT[:, a * P:(a + 1) * P], sc[:, k % 2, a * P:(a + 1) * P], ident)
                last.then_inc(t_done, 1)

            def values(k):
                un = units[k]
                par, h, i, w = un["g"] % 2, un["h"], un["i"], un["w"]
                hs = slice(h * P, (h + 1) * P)
                if i == 0:
                    if un["head"] >= 1:
                        pe.wait_ge(o_dve, un["head"])
                    if un["kind"] == "ret" and un["ret"] >= 1:
                        pe.wait_ge(o_act, un["ret"])
                if un["kind"] == "ret":
                    pe.wait_ge(s_read, k + 1)
                    last = pe.matmul(PO[:, i * P:S], v[:, par, i, hs], sc[:, k % 2, 0:w],
                                     start=(i == 0), stop=(i == NT - 1))
                else:
                    pe.wait_ge(t_copied, un["soft"] + 1)
                    for a in range(w // P):
                        lhs = (vm[:, a, (2 * un["g"] + h) * P:(2 * un["g"] + h + 1) * P] if un["mem"]
                               else v[:, par, a, hs])
                        last = pe.matmul(PO[:, i * P:(i + 1) * P], lhs, pT[:, k % 2, a * P:(a + 1) * P],
                                         start=(a == 0), stop=(a == w // P - 1))
                last.then_inc(v_done, 1)

            def slot(k, layer):
                if in_layer(k, layer):
                    scores(k)
                if in_layer(k - 2, layer):
                    values(k - 2)
                if in_layer(k - 1, layer) and units[k - 1]["kind"] != "ret":
                    transposes(k - 1)
                if in_layer(k - 3, layer) and units[k - 3]["kind"] == "ret" and units[k - 3]["i"] == NT - 1:
                    pe.wait_ge(o_act, units[k - 3]["ret"] + 1)
                    if units[k - 3]["ret"] >= 1:
                        pe.wait_ge(sd_done, units[k - 3]["ret"])
                    else:
                        pe.wait_ge(t_copied, nsoft_of(1))
                    pe.matmul(PT[:], cst[:, C_ONE:C_ONE + P], sq[:], start=True, stop=True).then_inc(ms_done, 1)

            def decay_sums():
                pe.wait_ge(d_gate, 1)
                pe.matmul(PB[0][:, 0:16], cst[:, C_TRI:C_TRI + P], lg, start=True, stop=True)
                for c in range(4):
                    last = pe.matmul(PB[1][0:4, c * P:(c + 1) * P], gs[:, 96 + 4 * c:100 + 4 * c],
                                     cst[:, C_TRI:C_TRI + P], start=True, stop=True)
                last.then_inc(d_cum, 1)

            def sums(s):
                if s in norm_steps:
                    r = norm_steps.index(s)
                    c0 = C_ONE if r < 8 else C_BD
                    pe.wait_ge(q_ready, r + 1)
                    if r >= 2:
                        pe.wait_ge(q_sd, r - 1)
                    pe.matmul(PJ[s % 2][:, S:2 * S], cst[:, c0:c0 + P], sq2[:, r % 2, :],
                              start=True, stop=True).then_inc(q_sum, 1)

            def delta_net():
                H4 = [slice(h * P, (h + 1) * P) for h in range(4)]
                pe.wait_ge(q_fin, 12)
                for a, src in enumerate((gv, gk)):
                    for c in range(4):
                        if a:
                            pe.wait_ge(g_vn, c + 1)
                        for h in range(4):
                            last = pe.transpose(PB[c][:, H4[h]], src[:, h, c * P:(c + 1) * P], ident)
                        last.then_inc(g_tr, 1)
                for c in range(4):
                    cs = slice(c * P, (c + 1) * P)
                    pe.wait_ge(g_kg, c + 1)
                    for h in range(4):
                        last = pe.matmul(PB[c][:, H4[h]], gk[:, h, cs], gk[:, h, cs], start=True, stop=True)
                    last.then_inc(g_kk, 1)
                n = 0
                for l in range(NLVL):
                    for c in range(4):
                        pe.wait_ge(g_bt, n + 1)
                        pe.wait_ge(g_tup, n + 1)
                        for h in range(4):
                            last = pe.matmul(PB[c][:, H4[h]], bt[:, n % 2, H4[h]], T_[:, c, H4[h]],
                                             start=True, stop=True)
                        last.then_inc(g_umm, 1)
                        n += 1
                    n -= 4
                    for c in range(4):
                        pe.wait_ge(g_uc, n + 1)
                        if l < NLVL - 1:
                            for h in range(4):
                                pe.matmul(PJ[c // 2][:, (c % 2) * S + h * P:(c % 2) * S + (h + 1) * P],
                                          TT[:, c, H4[h]], U[:, c, H4[h]], start=True, stop=True)
                        for h in range(4):
                            last = pe.matmul(PB[c][:, H4[h]], U[:, c, H4[h]], TT[:, c, H4[h]], start=True, stop=True)
                        last.then_inc(g_tmm, 1)
                        n += 1
                for c in range(4):
                    pe.wait_ge(g_tup, 4 * NLVL + c + 1)
                    for h in range(4):
                        last = pe.matmul(PB[c][:, H4[h]], kg[:, c, H4[h]], TT[:, c, H4[h]], start=True, stop=True)
                    last.then_inc(g_nmm, 1)
                for c in range(4):
                    cs = slice(c * P, (c + 1) * P)
                    for h in range(4):
                        last = pe.matmul(PJ[c // 2][:, (c % 2) * S + h * P:(c % 2) * S + (h + 1) * P],
                                         gk[:, h, cs], gq[:, h, cs], start=True, stop=True)
                    last.then_inc(g_imm, 1)
                for c in range(4):
                    cs = slice(c * P, (c + 1) * P)
                    if c == 0:
                        pe.wait_ge(g_nw, 4)
                    else:
                        pe.wait_ge(g_se, c)
                    for h in range(4):
                        last = pe.matmul(PB[0][:, H4[h]], TT[:, c, H4[h]], vn[:, c, H4[h]], start=True, stop=(c == 0))
                        if c:
                            last = pe.matmul(PB[0][:, H4[h]], nw[:, c, H4[h]], SS[:, c % 2, H4[h]],
                                             start=False, stop=True)
                    last.then_inc(g_vmm, 1)
                    pe.wait_ge(g_vne, c + 1)
                    if c < 3:
                        for h in range(4):
                            last = pe.matmul(PB[2][:, H4[h]], kd[:, c, H4[h]], vnw[:, c % 2, H4[h]],
                                             start=True, stop=True)
                        last.then_inc(g_smm, 1)
                    if c == 0:
                        pe.wait_ge(g_qd, 1)
                    else:
                        pe.wait_ge(g_oe, c)
                    for h in range(4):
                        if c:
                            pe.matmul(PB[1][:, H4[h]], SS[:, c % 2, H4[h]], gq[:, h, cs], start=True, stop=False)
                        last = pe.matmul(PB[1][:, H4[h]], vnw[:, c % 2, H4[h]], iT[:, c, H4[h]],
                                         start=(c == 0), stop=True)
                    last.then_inc(g_omm, 1)
                for h in range(4):
                    pe.wait_ge(y_sq, h + 1)
                    pe.matmul(PB[h][:], cst[:, C_ONE:C_ONE + P], kg[:, h, :], start=True, stop=True).then_inc(y_ms, 1)

            pe.wait_ge(s_cst, 16)
            for s, st in enumerate(steps):
                L = st["layer"]
                if s == 0 or steps[s - 1]["layer"] != L:
                    norm_transpose(2 * L)
                    norm_transpose(2 * L + 1)
                    pe.wait_ge(n_lo, 2 * tiles_before[2 * L + 2])
                    if L == 0:
                        pe.wait_ge(s_wn, 2)
                        narrow(0, N_F, NMAIN)
                    if L == 2:
                        narrow(1, N_BA, 8)
                if s == gdn_step:
                    delta_net()
                middle = st["slots"][:1] if len(st["slots"]) == 2 and st["kind"] in ("q", "z") else []
                products(s, middle)
                r = s - layer_first[L]
                if L == 0 and r == 1:
                    narrow_transpose(0, NMAIN).then_inc(f_mm, 1)
                if L == 0 and r == 4:
                    forget_sums()
                if L == 2 and r == 1:
                    narrow_transpose(1, 8).then_inc(d_mm, 1)
                if L == 2 and r == 4:
                    decay_sums()
                if s >= 1 and steps[s - 1]["kind"] == "rqk":
                    pe.wait_ge(rr_ready, rope_no(s - 1) + 1)
                    pe.matmul(PJ[(s - 1) % 2][:, S:2 * S], cst[:, C_PERM:C_PERM + P],
                              (qT, kT)[steps[s - 1]["c"]][:, steps[s - 1]["g"] % 2, 1, :],
                              start=True, stop=True).then_inc(perm_done, 1)
                for k in st["slots"][len(middle):]:
                    slot(k, L)
                if L == 2:
                    sums(s - 1)

            norm_transpose(6)
            pe.wait_ge(n_lo, 2 * tiles_before[7])
            narrow(2, N_R, 36)
            narrow_transpose(2, 36).then_inc(r_mm, 1)
            pe.wait_ge(r_E, 1)
            for t in range(NT + 1):
                js = range(t + 1) if t < NT else range(NT)
                for j in js:
                    c0 = C_STRI if j == t else C_ONE
                    last = pe.matmul(PB[1][:, t * NE:(t + 1) * NE], cst[:, c0:c0 + P], fld["E"][:, j, :],
                                     start=(j == 0), stop=(j == js[-1]))
            last.then_inc(r_rk, 1)

            def block_transpose(b):
                pe.wait_ge(x_g, b * 16 + 16)
                for k in range(KD):
                    last = pe.matmul(PB[0][:, k * CAP:(k + 1) * CAP], xs[0:CAP, k * P:(k + 1) * P],
                                     ident[0:CAP, 0:CAP], start=True, stop=True)
                last.then_inc(x_tr, 1)

            def gate_up(e, slots, lo, base):
                pe.wait_ge(x_lo, e + 1)
                for j in range(4):
                    pe.wait_ge(lo, base + (j + 1))
                    dst = PJ[0][0:CAP, FF * (j // 2):FF * (j // 2 + 1)]
                    for k in range(4):
                        kk = 4 * (j % 2) + k
                        ws = slice(k * FF, (k + 1) * FF)
                        last = mm3(pe, dst, (xT_hi[:, kk, :], xT_lo[:, kk, :]),
                                   (w_hi[:, slots[j], ws], w_lo[:, slots[j], ws]), kk == 0, kk == KD - 1)
                    last.then_inc(mm_of[lo.name], 1)

            def hidden_transpose(e):
                pe.wait_ge(h_mid, e + 1)
                for k in range(4):
                    last = pe.matmul(PB[2][:, k * CAP:(k + 1) * CAP], mid[0:CAP, k * P:(k + 1) * P],
                                     ident[0:CAP, 0:CAP], start=True, stop=True)
                last.then_inc(h_tr, 1)

            def down(e, slots, lo, base):
                pe.wait_ge(h_lo, e + 1)
                for j in range(2):
                    pe.wait_ge(lo, base + (j + 1))
                    for k in range(2):
                        kk = 2 * j + k
                        for hf in range(2):
                            ws = slice(k * D + hf * S, k * D + (hf + 1) * S)
                            last = mm3(pe, PJ[1][0:CAP, hf * S:(hf + 1) * S], (mT_h[:, kk, :], mT_l[:, kk, :]),
                                       (w_hi[:, slots[j], ws], w_lo[:, slots[j], ws]), kk == 0, kk == 3)
                    last.then_inc(mm_of[lo.name], 1)

            mm_of = {m_lo.name: m_mm, o_lo.name: o_mm}
            sl = [(4 + j) % SPLIT for j in range(6)]
            pe.wait_ge(r_dst, 1)
            block_transpose(0)
            gate_up(0, [j % SPLIT for j in range(4)], m_lo, 0)
            block_transpose(1)
            with pe.Fori(1, NE) as e:
                hidden_transpose(e - 1)
                gate_up(e, sl[0:4], m_lo, e * 6 + (4 - 6))
                block_transpose(e + 1)
                down(e - 1, sl[4:6], m_lo, e * 6 + (8 - 6))
            hidden_transpose(NE - 1)
            down(NE - 1, sl[0:2], m_lo, 6 * NE - 2)
            with pe.register("pe_nov") as r:
                pe.reg_load(r, ov[0:1, NOV:NOV + 1])
                with pe.If(pe.snap(r) > 0):
                    with pe.Fori(0, NOV) as b:
                        gate_up(b + NE, [0, 1, 2, 0], o_lo, b * 6)
                        block_transpose(b + (NE + 1))
                        hidden_transpose(b + NE)
                        down(b + NE, [1, 2], o_lo, b * 6 + 4)


def constants(np):
    f = np.float32
    i, j = np.arange(P)[:, None], np.arange(P)[None, :]
    perm = np.zeros((P, P), f)
    for b in (0, 64):
        for n in range(32):
            perm[b + 32 + n, b + n] = -1
            perm[b + n, b + 32 + n] = 1
    parts = [np.eye(P), np.ones((P, P)), i <= j, i < j, np.where(j <= i, 0, NEG), np.where(i <= j, 0, NEG),
             perm, i // 64 == j // 64]
    for l in range(NLVL):
        s = 1 << l
        parts.append((i // (2 * s) == j // (2 * s)) & (i // s % 2 == 0) & (j // s % 2 == 1))
    cst = np.concatenate([np.asarray(p, f) for p in parts], axis=1)
    inv = (1.0 / (f(10000.0) ** (np.arange(32, dtype=f) / f(32)))).astype(f)
    ang = (np.arange(S, dtype=f)[None, :] * inv[:, None]).astype(f)
    rope = np.stack([np.tile(np.cos(ang), (4, 1)), np.tile(np.sin(ang), (4, 1))]).astype(f)
    lg = np.log1p(-np.exp2(-5.0 - np.arange(NMAIN)))
    dist = np.arange(S)[None, None, :] - np.arange(P)[:, None, None]
    decay = np.where(dist >= 0, np.exp(lg[None, :, None] * np.maximum(dist, 0)), 0).astype(f)
    return cst, rope, decay


def kernel(**inputs):
    import numpy as np
    import concourse.bacc as bacc
    from concourse.bass_utils import run_bass_kernel_spmd

    def vec(name, n):
        a = np.asarray(inputs[name])
        return a.reshape(-1, n, P).transpose(2, 1, 0).reshape(P, -1)

    g = {k: np.asarray(a) for k, a in inputs.items()}
    cst, rope, decay = constants(np)
    arrays = {
        "x": g["x"][0], "mem": g["mem"][0], "fox_w_in": g["fox_w_in"][0], "ret_w_in": g["ret_w_in"][0],
        "w_mem_kv": g["w_mem_kv"], "w_out": g["w_out"], "w_in_2": g["w_in_2"][0], "w_out_2": g["w_out_2"][0],
        "w_gate": g["w_gate_2"][0], "w_up": g["w_up_2"][0], "w_down": g["w_down_2"][0],
        "gains": np.concatenate([g["norm_g"], g["mem_norm_g"][None], g["mix_norm_g_2"], g["ffn_norm_g_2"],
                                 g["final_norm_g_2"][None], g["final_norm_g"][None]]),
        "wn": np.concatenate([g["fox_w_in"][0][:, 3 * MAIN_W:3 * MAIN_W + NMAIN], g["w_in_2"][0][:, 3584:3592],
                              g["router_group_w_2"][0], g["router_expert_w_2"][0]], axis=1),
        "rows": np.concatenate([g["fox_b_f"], g["dn_a_log_2"], g["dn_dt_bias_2"]], axis=1),
        "vecs": np.concatenate([vec("dn_conv_w_2", 12), vec("conv_a_w_2", 4), vec("conv_a_norm_g_2", 4),
                                vec("dn_norm_g_2", 1)], axis=1),
        "cst": cst, "rope": rope, "decay": decay,
        "rowc": np.concatenate([np.arange(NG, 0, -1), np.arange(EPG, 0, -1), np.arange(NE),
                                ]).astype(np.float32)[None],
    }
    arrays = {k: np.ascontiguousarray(a) for k, a in arrays.items()}
    nc = bacc.Bacc("TRN2", target_bir_lowering=False, num_devices=1)
    A = {k: nc.dram_tensor("in_" + k, a.shape, mybir.dt.from_np(a.dtype), kind="ExternalInput").ap()
         for k, a in arrays.items()}
    out = nc.dram_tensor("out_0", (1, S, D), F32, kind="ExternalOutput").ap()
    A["scr_tab"] = nc.dram_tensor("scr_tab", (CAP * NB, 1), I32).ap()
    A["scr_h"] = nc.dram_tensor("scr_h", (S, D), F32).ap()
    A["scr_y"] = nc.dram_tensor("scr_y", ((NE + NOV) * CAP, D), F32).ap()
    A["scr_g"] = nc.dram_tensor("scr_g", (4, S), F32).ap()
    A["scr_c"] = nc.dram_tensor("scr_c", (NMAIN, S), F32).ap()
    program(nc, A, out, DEBUG)
    r = run_bass_kernel_spmd(nc, [{"in_" + k: a for k, a in arrays.items()}], core_ids=[0])
    return r.results[0]["out_0"]


DEBUG = 3
```
